# Optimizing a Trainium2 kernel written in Bass

```python
import numpy as np
import jax
import jax.numpy as jnp
from jax import lax

D_MODEL = 1024
BATCH = 1
SEQ = 512
DEPTH = 1

HEAD_DIM = 64
N_MIXERS = 4
GROUP_WIDTH = D_MODEL // N_MIXERS
N_GROUP_HEADS = GROUP_WIDTH // HEAD_DIM
BLOCK = 128
RMS_EPS = 1e-6

SWA_WINDOW = 128
SWA_KV_HEADS = N_GROUP_HEADS // 2

POOL_WINDOWS = (2, 4, 8, 16)
POOL_GROUP_CH = GROUP_WIDTH // len(POOL_WINDOWS)

CMP_LEN = 32
CMP_STRIDE = 16
SEL_BLOCK = 64
NSA_TOP_N = 16
NSA_WINDOW = 512
NSA_FORCE = 1e4

DN_CONV = 4
DN_CHUNK = 64

N_EXPERT_GROUPS = 4
EXPERTS_PER_GROUP = 4
EXPERT_TOP_K = 2
D_EXPERT = D_MODEL // 2

IN_SIZES = (GROUP_WIDTH, SWA_KV_HEADS * HEAD_DIM, SWA_KV_HEADS * HEAD_DIM,
            GROUP_WIDTH,
            GROUP_WIDTH, 6 * HEAD_DIM, 3 * N_GROUP_HEADS,
            3 * GROUP_WIDTH, GROUP_WIDTH, N_GROUP_HEADS, N_GROUP_HEADS)
IN_WIDTH = sum(IN_SIZES)
IN_OFFSETS = tuple(int(o) for o in np.cumsum(IN_SIZES)[:-1])

kernel_name = 'hybrid_parallel_heads_hier_moe'

F32 = jnp.float32

def rms_norm(x, gain):
    x32 = x.astype(F32)
    y = x32 * lax.rsqrt(jnp.mean(x32 * x32, axis=-1, keepdims=True) + RMS_EPS)
    return (y * gain.astype(F32)).astype(x.dtype)

def l2_normalize(t):
    return t * lax.rsqrt(jnp.sum(t * t, axis=-1, keepdims=True) + 1e-6)

def masked_softmax(s, mask):
    s = jnp.where(mask, s, -jnp.inf)
    m = jnp.max(s, axis=-1, keepdims=True)
    m = jnp.where(jnp.isfinite(m), m, 0.0)
    p = jnp.where(mask, jnp.exp(s - m), 0.0)
    d = jnp.sum(p, axis=-1, keepdims=True)
    return p / jnp.where(d > 0, d, 1.0)

def banded_attention(q, k, v, window, sink=None):
    b, s, hq, dh = q.shape
    hkv = k.shape[2]
    grp = hq // hkv
    nb = s // BLOCK
    span = window + BLOCK
    qb = q.reshape(b, nb, BLOCK, hkv, grp, dh)
    pad = ((0, 0), (window, 0), (0, 0), (0, 0))
    idx = jnp.arange(nb)[:, None] * BLOCK + jnp.arange(span)[None, :]
    kb = jnp.pad(k, pad)[:, idx]
    vb = jnp.pad(v, pad)[:, idx]
    tq = (jnp.arange(nb)[:, None] * BLOCK + jnp.arange(BLOCK)[None, :])[:, :, None]
    tk = (idx - window)[:, None, :]
    mask = (tk <= tq) & (tk > tq - window) & (tk >= 0)
    sc = jnp.einsum('bnqhgd,bnkhd->bnhgqk', qb, kb).astype(F32) * dh ** -0.5
    sc = jnp.where(mask[None, :, None, None], sc, -jnp.inf)
    m = jnp.max(sc, axis=-1, keepdims=True)
    if sink is not None:
        sink_l = sink.astype(F32).reshape(1, 1, hkv, grp, 1, 1)
        m = jnp.maximum(m, sink_l)
        p = jnp.exp(sc - m)
        denom = jnp.sum(p, axis=-1, keepdims=True) + jnp.exp(sink_l - m)
    else:
        p = jnp.exp(sc - m)
        denom = jnp.sum(p, axis=-1, keepdims=True)
    o = jnp.einsum('bnhgqk,bnkhd->bnqhgd', p / denom, vb.astype(F32))
    return o.reshape(b, s, hq, dh).astype(q.dtype)

def multiscale_pool(u, w_pool, pool_scale):
    b, s, _ = u.shape
    u32 = u.astype(F32)
    cs = jnp.cumsum(u32, axis=1)
    pos = jnp.arange(s)
    outs = []
    for gi, w in enumerate(POOL_WINDOWS):
        sl = slice(gi * POOL_GROUP_CH, (gi + 1) * POOL_GROUP_CH)
        c_g = cs[..., sl]
        lower = jnp.pad(c_g[:, :s - w], ((0, 0), (w, 0), (0, 0)))
        cnt = jnp.minimum(pos + 1, w).astype(F32)[None, :, None]
        outs.append((c_g - lower) / cnt - u32[..., sl])
    d = jnp.stack(outs, axis=2)
    y = jnp.einsum('bsgc,gcd->bsgd', d, w_pool.astype(F32)).reshape(b, s, -1) * pool_scale.astype(F32)
    return y.astype(u.dtype)

def nsa_attention(q, kv, gate_raw, cmp_pos, cmp_w1, cmp_w2):
    b, s, h, dh = q.shape
    k_cmp, v_cmp, k_sel, v_sel, k_win, v_win = jnp.split(kv, 6, axis=-1)
    n_cmp = (s - CMP_LEN) // CMP_STRIDE + 1
    n_sel = s // SEL_BLOCK
    n_top = min(NSA_TOP_N, n_sel)
    cmp_start = jnp.arange(n_cmp) * CMP_STRIDE
    win_idx = cmp_start[:, None] + jnp.arange(CMP_LEN)[None, :]

    def compress(t, pos, w1, w2):
        blocks = (t[:, win_idx] + pos).reshape(b, n_cmp, CMP_LEN * dh)
        return jax.nn.silu(blocks @ w1) @ w2

    kc = compress(k_cmp, cmp_pos[0], cmp_w1[0], cmp_w2[0]).astype(F32)
    vc = compress(v_cmp, cmp_pos[1], cmp_w1[1], cmp_w2[1]).astype(F32)
    sel_start = jnp.arange(n_sel) * SEL_BLOCK
    cover = jnp.maximum(jnp.minimum(cmp_start[:, None] + CMP_LEN, sel_start[None, :] + SEL_BLOCK)
                        - jnp.maximum(cmp_start[:, None], sel_start[None, :]), 0).astype(F32) / CMP_LEN
    cmp_end = cmp_start + CMP_LEN - 1
    kb = k_sel.reshape(b, n_sel, SEL_BLOCK, dh)
    vb = v_sel.reshape(b, n_sel, SEL_BLOCK, dh)
    blk = jnp.arange(n_sel)
    scale = dh ** -0.5

    def query_block(i):
        t = i * BLOCK + jnp.arange(BLOCK)
        qi = lax.dynamic_slice_in_dim(q, i * BLOCK, BLOCK, axis=1).astype(F32)
        p_c = masked_softmax(jnp.einsum('bqhd,bnd->bhqn', qi, kc) * scale, cmp_end[None, :] <= t[:, None])
        o_c = jnp.einsum('bhqn,bnd->bqhd', p_c, vc)
        importance = jnp.einsum('bhqn,nj->bqj', p_c, cover)
        cur = (t // SEL_BLOCK)[:, None]
        forced = (blk[None, :] == 0) | (blk[None, :] == cur) | (blk[None, :] == cur - 1)
        causal = blk[None, :] * SEL_BLOCK <= t[:, None]
        score = jnp.where(causal, jnp.where(forced, NSA_FORCE, importance), -jnp.inf)
        _, idx = lax.top_k(score, n_top)
        kg = jax.vmap(lambda a, ix: a[ix])(kb, idx).astype(F32)
        vg = jax.vmap(lambda a, ix: a[ix])(vb, idx).astype(F32)
        key_pos = idx[..., None] * SEL_BLOCK + jnp.arange(SEL_BLOCK)
        m_s = (key_pos <= t[None, :, None, None]).reshape(b, BLOCK, 1, n_top * SEL_BLOCK)
        s_s = jnp.einsum('bqhd,bqnkd->bqhnk', qi, kg).reshape(b, BLOCK, h, n_top * SEL_BLOCK) * scale
        p_s = masked_softmax(s_s, m_s)
        o_s = jnp.einsum('bqhm,bqmd->bqhd', p_s, vg.reshape(b, BLOCK, n_top * SEL_BLOCK, dh))
        return o_c, o_s

    o_c, o_s = lax.map(query_block, jnp.arange(s // BLOCK))
    to_seq = lambda o: jnp.moveaxis(o, 0, 1).reshape(b, s, h, dh)
    o_w = banded_attention(q, k_win[:, :, None], v_win[:, :, None], NSA_WINDOW).astype(F32)
    gates = jax.nn.sigmoid(gate_raw.astype(F32)).reshape(b, s, h, 3, 1)
    out = gates[:, :, :, 0] * to_seq(o_c) + gates[:, :, :, 1] * to_seq(o_s) + gates[:, :, :, 2] * o_w
    return out.astype(q.dtype)

def gated_delta_rule(q, k, v, g, beta):
    b, s, h, dk = q.shape
    dv = v.shape[-1]
    n = s // DN_CHUNK
    cl = DN_CHUNK

    def chunks(t):
        return jnp.moveaxis(t.reshape(b, n, cl, h, -1), 3, 1)

    q, k, v = chunks(q), chunks(k), chunks(v)
    g = jnp.cumsum(jnp.moveaxis(g.reshape(b, n, cl, h), 3, 1), axis=-1)
    beta = jnp.moveaxis(beta.reshape(b, n, cl, h), 3, 1)[..., None]
    k_beta = k * beta
    v_beta = v * beta
    causal = jnp.tril(jnp.ones((cl, cl), bool))
    strict = jnp.tril(jnp.ones((cl, cl), bool), -1)
    decay = jnp.exp(jnp.where(causal, g[..., :, None] - g[..., None, :], -jnp.inf))
    lower = jnp.where(strict, jnp.einsum('bhnid,bhnjd->bhnij', k_beta, k) * decay, 0.0)
    eye = jnp.eye(cl, dtype=q.dtype)
    t_inv = lax.linalg.triangular_solve(eye + lower, jnp.broadcast_to(eye, lower.shape),
                                        left_side=True, lower=True, unit_diagonal=True)
    u = t_inv @ v_beta
    w = t_inv @ (k_beta * jnp.exp(g)[..., None])
    intra = jnp.where(causal, jnp.einsum('bhnid,bhnjd->bhnij', q, k) * decay, 0.0)
    q_dec = q * jnp.exp(g)[..., None]
    k_dec = k * jnp.exp(g[..., -1:] - g)[..., None]
    chunk_decay = jnp.exp(g[..., -1])

    def step(state, xs):
        u_i, w_i, qd_i, kd_i, a_i, cd_i = xs
        v_new = u_i - w_i @ state
        o_i = qd_i @ state + a_i @ v_new
        state = state * cd_i[..., None, None] + jnp.swapaxes(kd_i, -1, -2) @ v_new
        return state, o_i

    xs = tuple(jnp.moveaxis(t, 2, 0) for t in (u, w, q_dec, k_dec, intra, chunk_decay))
    state0 = jnp.zeros((b, h, dk, dv), q.dtype)
    _, o = lax.scan(step, state0, xs)
    return jnp.moveaxis(o, 0, 2).transpose(0, 2, 3, 1, 4).reshape(b, s, h, dv)

def gated_deltanet(qkv, z, beta_raw, a_raw, conv_w, a_log, dt_bias, norm_w):
    b, s, ch = qkv.shape
    qkv = jax.nn.silu(lax.conv_general_dilated(qkv, conv_w[:, None, :], (1,), [(DN_CONV - 1, 0)],
                                               dimension_numbers=('NWC', 'WIO', 'NWC'),
                                               feature_group_count=ch))
    q, k, v = (t.reshape(b, s, N_GROUP_HEADS, HEAD_DIM).astype(F32) for t in jnp.split(qkv, 3, axis=-1))
    q = l2_normalize(q) * HEAD_DIM ** -0.5
    k = l2_normalize(k)
    beta = jax.nn.sigmoid(beta_raw.astype(F32))
    g = -jnp.exp(a_log.astype(F32)) * jax.nn.softplus(a_raw.astype(F32) + dt_bias.astype(F32))
    o = gated_delta_rule(q, k, v, g, beta)
    o = o * lax.rsqrt(jnp.mean(o * o, axis=-1, keepdims=True) + RMS_EPS) * norm_w.astype(F32)
    o = o * jax.nn.silu(z.astype(F32).reshape(b, s, N_GROUP_HEADS, HEAD_DIM))
    return o.reshape(b, s, -1).astype(qkv.dtype)

def hybrid_mixer(h, w_in, w_out, attn_sink, w_pool, pool_scale, cmp_pos, cmp_w1, cmp_w2,
                 conv_w, a_log, dt_bias, dn_norm):
    b, s, _ = h.shape
    (a_q, a_k, a_v, pool_in, c_q, c_kv, c_gate,
     d_qkv, d_z, d_beta, d_a) = jnp.split(h @ w_in, IN_OFFSETS, axis=-1)
    heads = lambda t: t.reshape(b, s, -1, HEAD_DIM)
    y_a = banded_attention(heads(a_q), heads(a_k), heads(a_v), SWA_WINDOW, attn_sink)
    y_b = multiscale_pool(pool_in, w_pool, pool_scale)
    y_c = nsa_attention(heads(c_q), c_kv, c_gate, cmp_pos, cmp_w1, cmp_w2)
    y_d = gated_deltanet(d_qkv, d_z, d_beta, d_a, conv_w, a_log, dt_bias, dn_norm)
    y = jnp.concatenate([y_a.reshape(b, s, -1), y_b, y_c.reshape(b, s, -1), y_d], axis=-1)
    return y @ w_out

def hier_moe(h, w_rg, b_rg, w_re, b_re, w_gate, w_up, w_down):
    b, s, d = h.shape
    t = h.reshape(b * s, d)
    p_group = jax.nn.softmax((t @ w_rg + b_rg).astype(F32), axis=-1)
    pg_top, g_top = lax.top_k(p_group, 1)
    g_onehot = jax.nn.one_hot(g_top[:, 0], N_EXPERT_GROUPS, dtype=F32)
    logits_e = (t @ w_re + b_re).astype(F32).reshape(-1, N_EXPERT_GROUPS, EXPERTS_PER_GROUP)
    p_exp = jax.nn.softmax(jnp.einsum('nge,ng->ne', logits_e, g_onehot), axis=-1)
    pe_top, e_top = lax.top_k(p_exp, EXPERT_TOP_K)
    pe_top = pe_top / jnp.sum(pe_top, axis=-1, keepdims=True)
    w_e = jnp.einsum('nke,nk->ne', jax.nn.one_hot(e_top, EXPERTS_PER_GROUP, dtype=F32), pe_top) * pg_top
    combine = (g_onehot[:, :, None] * w_e[:, None, :]).astype(h.dtype)
    y = jnp.zeros_like(t)
    for gi in range(N_EXPERT_GROUPS):
        hid = jax.nn.silu(jnp.einsum('nd,edf->nef', t, w_gate[gi])) * jnp.einsum('nd,edf->nef', t, w_up[gi])
        y = y + jnp.einsum('nef,efd->nd', hid * combine[:, gi, :, None], w_down[gi])
    return y.reshape(b, s, d)

def setup_inputs(seed: int = 0) -> dict:
    key = jax.random.key(seed)
    keys = iter(jax.random.split(key, 40))

    def normal(shape, scale):
        return jax.random.normal(next(keys), shape, F32) * scale

    def gain(shape):
        return 1.0 + normal(shape, 0.02)

    L, D, H = DEPTH, D_MODEL, N_GROUP_HEADS
    G, EG, F = N_EXPERT_GROUPS, EXPERTS_PER_GROUP, D_EXPERT
    x = normal((BATCH, SEQ, D), 1.0)
    c = normal((BATCH, D), 1.0)
    dt = jax.random.uniform(next(keys), (L, H), F32, 1e-3, 1e-1)
    a_log = jnp.log(jax.random.uniform(next(keys), (L, H), F32, 1.0, 16.0))
    return {
        'x': x,
        'c': c,
        'norm_mix': gain((L, D)),
        'norm_ffn': gain((L, D)),
        'final_norm': gain((D,)),
        'w_ada': normal((L, D, 6 * D), 0.25 * D ** -0.5),
        'b_ada': normal((L, 6 * D), 0.02),
        'w_in': normal((L, D, IN_WIDTH), D ** -0.5),
        'w_out': normal((L, D, D), D ** -0.5),
        'attn_sink': normal((L, H), 0.5),
        'w_pool': normal((L, len(POOL_WINDOWS), POOL_GROUP_CH, POOL_GROUP_CH), POOL_GROUP_CH ** -0.5),
        'pool_scale': gain((L, GROUP_WIDTH)),
        'cmp_pos': normal((L, 2, CMP_LEN, HEAD_DIM), 0.02),
        'cmp_w1': normal((L, 2, CMP_LEN * HEAD_DIM, HEAD_DIM), (CMP_LEN * HEAD_DIM) ** -0.5),
        'cmp_w2': normal((L, 2, HEAD_DIM, HEAD_DIM), HEAD_DIM ** -0.5),
        'conv_w': normal((L, DN_CONV, 3 * GROUP_WIDTH), DN_CONV ** -0.5),
        'a_log': a_log,
        'dt_bias': jnp.log(jnp.expm1(dt)),
        'dn_norm': gain((L, HEAD_DIM)),
        'w_route_group': normal((L, D, G), D ** -0.5),
        'b_route_group': normal((L, G), 0.01),
        'w_route_expert': normal((L, D, G * EG), D ** -0.5),
        'b_route_expert': normal((L, G * EG), 0.01),
        'w_gate': normal((L, G, EG, D, F), D ** -0.5),
        'w_up': normal((L, G, EG, D, F), D ** -0.5),
        'w_down': normal((L, G, EG, F, D), F ** -0.5),
    }

def reference(x, c, norm_mix, norm_ffn, final_norm, w_ada, b_ada, w_in, w_out, attn_sink, w_pool,
              pool_scale, cmp_pos, cmp_w1, cmp_w2, conv_w, a_log, dt_bias, dn_norm, w_route_group,
              b_route_group, w_route_expert, b_route_expert, w_gate, w_up, w_down):
    cond = jax.nn.silu(c)
    for l in range(DEPTH):
        mod = (cond @ w_ada[l] + b_ada[l])[:, None, :]
        sh1, sc1, g1, sh2, sc2, g2 = jnp.split(mod, 6, axis=-1)
        h = rms_norm(x, norm_mix[l]) * (1 + sc1) + sh1
        y = hybrid_mixer(h, w_in[l], w_out[l], attn_sink[l], w_pool[l], pool_scale[l], cmp_pos[l],
                         cmp_w1[l], cmp_w2[l], conv_w[l], a_log[l], dt_bias[l], dn_norm[l])
        x = x + g1 * y
        h = rms_norm(x, norm_ffn[l]) * (1 + sc2) + sh2
        x = x + g2 * hier_moe(h, w_route_group[l], b_route_group[l], w_route_expert[l],
                              b_route_expert[l], w_gate[l], w_up[l], w_down[l])
    return rms_norm(x, final_norm)


_drawn_inputs = setup_inputs


def setup_inputs(seed=0):
    import zlib

    import numpy as np

    out = dict(_drawn_inputs(seed))
    spreads = {}
    factors = {'norm_mix': 8.0,
     'norm_ffn': 8.0,
     'final_norm': 21.976,
     'b_ada': 4.124,
     'attn_sink': 200.0,
     'pool_scale': 8.0,
     'cmp_pos': 8.0,
     'cmp_w1': 5.591,
     'cmp_w2': 3.804,
     'a_log': 3.919,
     'dt_bias': 3.765,
     'dn_norm': 8.0,
     'b_route_group': 8.0,
     'b_route_expert': 28.956}
    for name, (base, spread) in spreads.items():
        noise = np.random.default_rng([zlib.crc32(name.encode()), seed]).standard_normal(out[name].shape)
        drawn = base * np.exp(spread * noise) if base else spread * noise
        out[name] = jnp.asarray(drawn.astype(out[name].dtype))
    for name, factor in factors.items():
        out[name] = (out[name] * factor).astype(out[name].dtype)
    return out
```

```python
from contextlib import ExitStack

import concourse.bass as bass
from concourse import mybir

F32 = mybir.dt.float32
BF16 = mybir.dt.bfloat16
I32 = mybir.dt.int32
U32 = mybir.dt.uint32
ALU = mybir.AluOpType
ACT = mybir.ActivationFunctionType
AX = mybir.AxisListType

P = 128
D = 1024
KT = D // P
S = 512
ST = S // P
HD = 64
H = 4
GW = 256
IN_SIZES = dict(aq=256, ak=128, av=128, pool=256, cq=256, ckv=384, cg=12, dqkv=768, dz=256, db=4, da=4)
OFF = {}
_o = 0
for _n, _w in IN_SIZES.items():
    OFF[_n] = _o
    _o += _w
IN_W = _o
CONV = 4
POOLW = (2, 4, 8, 16)
CMP_LEN, CMP_STRIDE = 32, 16
NCMP = (S - CMP_LEN) // CMP_STRIDE + 1
CH = 64
NCH = S // CH
G, EG = 4, 4
E = G * EG
F = 512
FT = F // P
EXTRA = 7
ROWS = (E + EXTRA) * P
EPS = 1e-6
NEG = -1e30
ZBA = 256 + 8
NTOK = ZBA


class Link:

    def __init__(self, eng, done):
        self.eng, self.done, self.n = eng, done, 0

    def __call__(self, ins):
        self.n += 1
        ins.then_inc(self.done, 1)
        self.eng.wait_ge(self.done, self.n)


def sbuf_map(nc):
    base = 16512
    ctx_tensors = {}

    def at(name, off, shape, dt=F32):
        n = 4 if dt in (F32, I32, U32) else 2
        for x in shape[1:]:
            n *= x
        assert base + off + n <= 229368, (name, off, n)
        ctx_tensors[name] = nc.alloc_sbuf_tensor_at(name, shape, dt, offset=base + off)
        spans.append((name, off, n))
        return off + (n + 31) // 32 * 32

    spans = []
    K = 1024
    R0 = 0
    at("ada", R0, [P, 2, KT, 512])
    at("gu0", R0, [P, 2, KT, F])
    R1 = 32 * K
    at("win", R1, [P, KT, IN_W])
    at("gu1", R1, [P, 2, KT, F])
    at("dn0", R1 + 32 * K, [P, FT, D])
    at("dn1", R1 + 48 * K, [P, FT, D])
    at("w1", R1, [P, CMP_LEN, HD])
    o = at("kpos", R1 + 8 * K, [P, 2, S])
    o = at("w2", o, [P, HD])
    o = at("hid", o, [P, 32])
    o = at("hsig", o, [P, 32])
    at("wout", R1, [P, KT, D])
    o = R1 + 32 * K
    for n in ("qn", "qd", "kn", "kbe", "kd", "vb"):
        o = at(n, o, [P, ST, GW])
    for n in ("qT", "qdT", "kT", "wT"):
        o = at(n, o, [HD, H, P])
    for n in ("asl", "dec", "low", "tt", "uu", "cc", "yy", "inT"):
        o = at(n, o, [P, H, P])
    assert o <= R1 + 80 * K
    at("pa", R1 + 40 * K, [P, 2, S])
    at("pb", R1 + 44 * K, [P, 2, S])
    at("pTr", R1 + 48 * K, [P, 2, ST, S])
    at("pd", R1 + 64 * K, [P, 2, S])
    at("osb", R1 + 32 * K, [P, ST, GW])
    at("x2", R1 + 64 * K, [P, ST, D])
    at("y1", R1, [P, ST, D])
    at("y2", R1 + 16 * K, [P, ST, D])
    RX = R1 + 80 * K
    at("x", RX, [P, ST, D])
    at("dtok", RX, [P, ST, 3 * GW])
    at("xr", RX, [P, 2, D])
    at("sqs", RX + 8 * K, [P, D])
    at("g2b", RX + 12 * K, [P, D])
    RN = RX + 16 * K
    at("xn", RN, [P, ST, D])
    o = at("cin", RN, [P, 2, S + CONV])
    o = at("cout", o, [P, 2, S])
    at("pr", RN, [P, 2, S])
    at("xn2", RN, [P, 2, D])
    at("x2T", RN + 8 * K, [P, KT, P])
    at("fnb", RN + 12 * K, [P, D])
    at("g1b", RN + 12 * K, [P, D])
    RH = RN + 16 * K
    at("hT", RH, [P, KT, S])
    at("yT", RH, [P, KT, S])
    o = at("hidm", RH, [P, F])
    o = at("hidT", o, [P, FT, P])
    o = at("yo", o, [P, D])
    o = at("sg", o, [P, F])
    o = RH + 16 * K
    RF = o
    o2 = at("xg", o, [P, 2, D])
    o2 = at("xgT", o2, [P, KT, P])
    for n, shape in (("lg", [P, ST, 20]), ("mx", [P, ST]), ("mn", [P, ST]), ("m1", [P, ST]), ("ed", [P, ST]),
                     ("t4", [P, ST, 4]), ("eg", [P, ST, 4]), ("ohg", [P, ST, 4]), ("oh1", [P, ST, 4]),
                     ("oh2", [P, ST, 4]), ("le", [P, ST, 4]), ("e16", [P, ST, E]), ("s16", [P, ST, E]),
                     ("M1", [P, ST, E]), ("M2", [P, ST, E]), ("chosen", [P, ST, E]), ("rank", [P, ST, E]),
                     ("count", [P, E]), ("xe", [P, E]), ("t16", [P, E]), ("incl", [P, E]), ("bb", [P, E]),
                     ("w1t", [P, ST]), ("w2t", [P, ST]), ("slotf", [P, 2, ST]), ("rf", [P, 8])):
        o2 = at(n, o2, shape)
    o2 = at("slot", o2, [P, 2, ST], U32)
    o2 = at("route_i", o2, [P, 8], I32)
    o2 = at("list", o2, [P, E + EXTRA], U32)
    for n, w in (("aqT", 2), ("akT", 1), ("plT", 2), ("cqT", 2), ("kcvT", 1), ("kselT", 1), ("kwinT", 1)):
        o = at(n, o, [P, w, S])
    o = at("va", o, [P, ST, P])
    o = at("vsw", o, [P, ST, P])
    o = at("cg", o, [P, ST, 12])
    o = at("zba", o, [P, ST, ZBA])
    o = at("idf", o, [P, P])
    o = at("idb", o, [P, P], BF16)
    o = at("negdiag", o, [P, P], BF16)
    o = at("negprev", o, [P, P], BF16)
    o = at("negcmp", o, [P, ST, 2, NCMP], BF16)
    o = at("negdec", o, [P, H, P], BF16)
    o = at("tri", o, [P, P])
    o = at("sl", o, [P, P])
    o = at("lev", o, [P, 6, P])
    o = at("small", o, [P, P])
    o = at("cols", o, [P, P])
    o = at("ones", o, [P, P])
    o = at("before", o, [P, P])
    o = at("zero", o, [P, P])
    o = at("state", o, [HD, GW])
    o = at("kc", o, [P, 32])
    o = at("vc", o, [P, HD])
    o = at("wr", o, [P, KT, 20])
    o = at("wrA", o, [P, KT, 20])
    o = at("rb", o, [P, 20])
    o = at("jm", o, [P, 4])
    o = at("e128", o, [P, E])
    o = at("jm_i", o, [P, 4], I32)
    o = at("e128_i", o, [P, E], I32)
    o = at("cnt_i", o, [P, 16], I32)
    o = at("tok", o, [P, ST], U32)
    o = at("zlist", o, [P, E + EXTRA], U32)
    o = at("u", o, [P, GW])
    o = at("vnew", o, [P, GW])
    o = at("wpool", o, [P, 2, HD])
    o = at("st", o, [P, 768])
    assert o <= 229368 - base, o
    return ctx_tensors


def build(nc, A, out):
    ctx = ExitStack()
    T = sbuf_map(nc)

    cut = {}
    n_st = [0]

    def stat(name, *shape, parts=P):
        w = 1
        for x in shape:
            w *= x
        v = T["st"][0:parts, n_st[0]:n_st[0] + w]
        n_st[0] += w
        assert n_st[0] <= 768, name
        if len(shape) == 2:
            v = v.rearrange("p (a b) -> p a b", a=shape[0])
        if len(shape) == 3:
            v = v.rearrange("p (a b c) -> p a b c", a=shape[0], b=shape[1])
        cut[name] = v
        return v

    cT, csil = stat("cT", KT), stat("csil", KT)
    mod = stat("mod", 48)
    A1, A2 = stat("A1", KT), stat("A2", KT)
    ss, rstd = stat("ss", ST), stat("rstd", ST)
    ss2, rstd2 = stat("ss2", ST), stat("rstd2", ST)
    sinkb, alogb, dtb = stat("sinkb", H), stat("alogb", H), stat("dtb", H)
    nsink = stat("nsink", H)
    beta, sp1, sp2, ga = (stat(n, ST, H) for n in ("beta", "sp1", "sp2", "ga"))
    negA = stat("negA", H)
    sqk, rqk = stat("sqk", ST, 8), stat("rqk", ST, 8)
    egc, kdec, rqe, rkbe, rkd = (stat(n, ST, H) for n in ("egc", "kdec", "rqe", "rkbe", "rkd"))
    cdec = stat("cdec", NCH, H)
    gate = stat("gate", ST, 12)
    sso, rso = stat("sso", ST, H), stat("rso", ST, H)
    ra = stat("ra", 4)
    poolrec = stat("poolrec", 16)
    nm = stat("nm", 2)
    den = stat("den", 2)
    rden = stat("rden", 2)
    esk = stat("esk", 2)
    nmc, denc, rdc = stat("nmc", H), stat("denc", H), stat("rdc", H)
    one, tiny = stat("one", 1), stat("tiny", 1)

    PS = [ctx.enter_context(nc.psum_tensor(f"ps{i}", [P, 512], F32)) for i in range(8)]
    sems = {}
    dve_link, pool_link = [None], [None]

    def sem(name):
        if name not in sems:
            sems[name] = ctx.enter_context(nc.semaphore(name))
        return sems[name]

    W = T["win"]
    idf, idb, cols = T["idf"], T["idb"], T["cols"]

    def in_cols(name, a=0, n=P):
        return lambda k: W[:, k, OFF[name] + a:OFF[name] + a + n]

    MOVED = {"aq": ((0, 0), (2, 1), (1, 2), (3, 3)), "ckv": ((2, 2), (4, 3), (3, 4), (5, 5))}

    block = ctx.enter_context(nc.Block())

    items = []
    for c in range(6):
        items.append(("cin", c, "act"))
    for i in range(ST):
        items.append(("zba", i, "dve" if i % 2 else "act"))
    for n, (name, j) in enumerate([("kcvT", 0), ("ksw", 0), ("cqT", 0), ("cqT", 1), ("aqT", 0), ("aqT", 1),
                                   ("akT", 0), ("plT", 0), ("plT", 1)]):
        items.append((name, j, "dve" if n % 2 else "act"))
    for i in range(ST):
        items.append(("v", i, "dve" if i % 2 else "act"))
    NI = len(items)
    PB = 6
    out_count = []
    seen = {"act": 0, "dve": 0}
    for it in items:
        seen[it[2]] += 1
        out_count.append((it[2], seen[it[2]]))
    ZBA_ITEMS = range(6, 6 + ST)

    def bank_empty(eng, n):
        who, k = out_count[n]
        eng.wait_ge(sem("proj_out_" + who), k)

    def all_out(eng, n):
        for who in ("act", "dve"):
            k = max([c for w, c in out_count[:n + 1] if w == who])
            eng.wait_ge(sem("proj_out_" + who), k)

    def empty_item(eng, scalar, n):
        name, j, _ = items[n]
        bank = PS[n % PB]
        signal = sem("proj_out_act" if scalar else "proj_out_dve")
        scale = 0.125 if name in ("cqT", "aqT") else 1.0
        src = bank[:, :]
        if name == "cin":
            if j >= 2:
                eng.wait_ge(sem("conv_done"), j - 1)
            dst = T["cin"][:, j % 2, CONV:CONV + S]
        elif name == "zba":
            dst, src = T["zba"][:, j, :], bank[:, 0:ZBA]
        elif name == "v":
            parts = [(T["va"][:, j, :], bank[:, 0:P]), (T["vsw"][:, j, :], bank[:, P:2 * P]),
                     (T["cg"][:, j, :], bank[:, 2 * P:2 * P + 12])]
        elif name != "ksw":
            dst = T[name][:, j, :]
        if name == "ksw":
            lo, hi = slice(0, HD), slice(HD, P)
            parts = [(T["kselT"][lo, 0, :], bank[lo, :]), (T["kselT"][hi, 0, :], bank[lo, :]),
                     (T["kwinT"][lo, 0, :], bank[hi, :]), (T["kwinT"][hi, 0, :], bank[hi, :])]
        elif name != "v":
            parts = [(dst, src)]
        for n_part, (d, s) in enumerate(parts):
            if scalar:
                ins = nc.scalar.activation(d, s, ACT.Copy, scale=scale)
            elif scale != 1.0:
                ins = nc.vector.tensor_scalar(d, s, scale, None, ALU.mult)
            else:
                ins = nc.vector.tensor_copy(d, s)
        ins.then_inc(signal, 1)

    HP_CHUNKS = 512 // P
    ada_v = A["w_ada"][0].rearrange("(p k) n -> p k n", k=KT)
    win_v = A["w_in"][0].rearrange("(k p) n -> p k n", p=P)
    WIN_GROUPS = [(OFF["dqkv"], OFF["dz"]), (OFF["dz"], IN_W), (OFF["ckv"], OFF["dqkv"]),
                  (OFF["cq"], OFF["ckv"]), (0, OFF["cq"])]
    GROUP_DMAS = (1, 1, 6, 1, 5)
    GROUP_OF = {"cin": 0, "zba": 1, "kcvT": 2, "ksw": 2, "cqT": 3, "aqT": 4, "akT": 4, "plT": 4, "v": 4}
    HPS = 12

    groups = []
    for pair in range(2):
        for kind in ("cmp", "sel", "win"):
            for h in (2 * pair, 2 * pair + 1):
                groups.append((kind, h))
    groups += [("swa", h) for h in range(H)]
    units = []
    for gi, (kind, h) in enumerate(groups):
        for i in range(ST):
            j0 = max(i - 1, 0) if kind == "swa" else 0
            nk = NCMP if kind == "cmp" else (i + 1 - j0) * P
            units.append((gi, kind, h, i, j0, nk))
    NU = len(units)

    def q_of(kind, h, i):
        tok = slice(i * P, (i + 1) * P)
        if kind == "swa":
            pb = HD * (h // 2)
            return T["aqT"][pb:pb + HD, h % 2, tok], pb
        pb = HD * (h % 2)
        return T["cqT"][pb:pb + HD, h // 2, tok], pb

    def y_bank(kind, h):
        return (6 if kind == "swa" else 4) + h // 2

    def compress_pe(pe):
        t = nc.tensor
        pe.wait_ge(sem("w1_in"), 64)
        pe.wait_ge(sem("kpos"), 1)
        pe.wait_ge(sem("wT_out"), ST)
        pe.wait_ge(sem("o_out"), ST)
        for l in range(CMP_LEN):
            for b, bank in enumerate((5, 6)):
                pb = slice(HD * b, HD * b + HD)
                ins = t.matmul(PS[bank][pb, 0:NCMP], T["w1"][pb, l, :],
                               T["kpos"][pb, l // CMP_STRIDE, l:l + CMP_STRIDE * (NCMP - 1) + 1:CMP_STRIDE],
                               start=(l == 0), stop=(l == CMP_LEN - 1))
        ins.then_inc(sem("hid_mm"), 1)
        pe.wait_ge(sem("hid"), 2)
        for b in range(2):
            t.matmul(PS[7][HD * b:HD * b + HD, 0:NCMP], T["w2"][0:HD], T["hid"][0:HD, 0:NCMP], start=True, stop=True)
        t.matmul(PS[0][0:NCMP, 0:HD], T["hid"][HD:P, 0:NCMP], T["w2"][HD:P], start=True,
                 stop=True).then_inc(sem("kc_mm"), 1)

    def pe_attention(pe):
        t = nc.tensor
        pe.wait_ge(sem("y_out"), 2)
        compress_pe(pe)
        pe.wait_ge(sem("kc_out"), 2)
        for u in range(NU + 5):
            if u < NU:
                gi, kind, h, i, j0, nk = units[u]
                q, pb = q_of(kind, h, i)
                if kind == "cmp":
                    keys = T["kc"][pb:pb + HD, 0:NCMP]
                else:
                    keys = {"sel": T["kselT"], "win": T["kwinT"], "swa": T["akT"]}[kind][pb:pb + HD, 0,
                                                                                       j0 * P:j0 * P + nk]
                if u >= 2:
                    pe.wait_ge(sem("exp"), u - 1)
                bank = PS[u % 2]
                t.matmul(bank[:, 0:nk], q, keys, start=True, stop=False)
                if kind == "cmp":
                    masks = [(bank[:, 0:NCMP], T["negcmp"][:, i, 0, :])]
                else:
                    masks = [(bank[:, nk - P:nk], T["negdiag"][:])]
                    if kind == "swa" and i:
                        masks.append((bank[:, 0:P], T["negprev"][:]))
                for n, (o, m) in enumerate(masks):
                    ins = t.matmul(o, idb[:], m, start=False, stop=(n == len(masks) - 1))
                ins.then_inc(sem("score_mm"), 1)
            if 2 <= u < NU + 2:
                w = u - 2
                gi, kind, h, i, j0, nk = units[w]
                pe.wait_ge(sem("prob"), w + 1)
                if w >= 2:
                    pe.wait_ge(sem("pT_out"), w - 1)
                if kind == "cmp":
                    ins = t.transpose(PS[2 + w % 2][0:NCMP, 0:P], T["pr"][:, w % 2, 0:NCMP], idf[:])
                else:
                    for b in range(nk // P):
                        ins = t.transpose(PS[2 + w % 2][:, b * P:(b + 1) * P], T["pr"][:, w % 2, b * P:(b + 1) * P], idf[:])
                ins.then_inc(sem("prob_tr"), 1)
            if 4 <= u < NU + 4 and units[u - 4][3] == ST - 1:
                gi, kind, h = units[u - 4][:3]
                pe.wait_ge(sem("pT_out"), u - 3)
                y = PS[y_bank(kind, h)][HD * (h % 2):HD * (h % 2) + HD]
                pT = T["pTr"][:, gi % 2]
                if kind == "cmp":
                    ins = t.matmul(y[:, :], T["vc"][0:NCMP, :], pT[0:NCMP, 0, :], start=True, stop=False)
                elif kind == "swa":
                    for i in range(ST):
                        js = [j for j in (i - 1, i) if j >= 0]
                        for j in js:
                            ins = t.matmul(y[:, i * P:(i + 1) * P], T["va"][:, j, HD * (h // 2):HD * (h // 2) + HD],
                                           pT[:, j, i * P:(i + 1) * P], start=(j == js[0]), stop=(j == i))
                else:
                    o = 0 if kind == "sel" else HD
                    for j in range(ST):
                        ins = t.matmul(y[:, j * P:S], T["vsw"][:, j, o:o + HD], pT[:, j, j * P:S], start=False,
                                       stop=(kind == "win" and j == ST - 1))
                ins.then_inc(sem("pv_mm"), 1)
        pe.wait_ge(sem("pool_d"), 1)
        pe.wait_ge(sem("pT_out"), NU)
        for c in range(2):
            for b in range(2):
                pb = slice(HD * b, HD * b + HD)
                ins = t.matmul(PS[2 * c + b][pb, :], T["wpool"][pb, c, :], T["pd"][pb, c, :], start=True, stop=True)
        ins.then_inc(sem("pool_mm"), 1)

    def dve_attention(dve):
        v = nc.vector
        link = dve_link[0]
        link(v.tensor_scalar(nsink, sinkb, -1.0, None, ALU.mult))
        dve.wait_ge(sem("masks"), 2)
        v.reciprocal(poolrec, poolrec).then_inc(sem("cnt"), 1)
        dve.wait_ge(sem("kc_mm"), 1)
        v.tensor_copy(T["kc"][:, 0:NCMP], PS[7][:, 0:NCMP]).then_inc(sem("kc_out"), 1)
        v.tensor_copy(T["vc"][0:NCMP, :], PS[0][0:NCMP, 0:HD]).then_inc(sem("kc_out"), 1)
        dve.wait_ge(sem("scalars"), 2)
        for u in range(NU + 1):
            if u < NU:
                gi, kind, h, i, j0, nk = units[u]
                dve.wait_ge(sem("score_mm"), u + 1)
                m = nm[:, u % 2:u % 2 + 1]
                if u >= 2:
                    dve.wait_ge(sem("exp"), u - 1)
                ins = v.tensor_reduce(m, PS[u % 2][:, 0:nk], AX.X, ALU.max, negate=True)
                if kind == "swa":
                    link(ins)
                    ins = v.tensor_scalar(m, m, nsink[:, h:h + 1], None, ALU.min)
                if kind == "cmp":
                    link(ins)
                    ins = v.tensor_scalar(m, m, 1e20, None, ALU.min)
                ins.then_inc(sem("max"), 1)
            if u >= 1:
                w = u - 1
                gi, kind, h, i, j0, nk = units[w]
                dve.wait_ge(sem("exp"), w + 1)
                d, r = den[:, w % 2:w % 2 + 1], rden[:, w % 2:w % 2 + 1]
                if kind == "swa":
                    link(v.tensor_tensor(d, d, esk[:, w % 2:w % 2 + 1], ALU.add))
                if kind == "cmp":
                    link(v.tensor_scalar(d, d, 0.5, None, ALU.max))
                link(v.reciprocal(r, d))
                p = T["pr"][:, w % 2, 0:nk]
                if kind == "swa":
                    ins = v.tensor_scalar(p, p, r, None, ALU.mult)
                else:
                    b = 3 * h + {"cmp": 0, "sel": 1, "win": 2}[kind]
                    ins = v.tensor_scalar(p, p, r, gate[:, i, b:b + 1], ALU.mult, ALU.mult)
                ins.then_inc(sem("prob"), 1)
        for c in range(2):
            dve.wait_ge(sem("pv_mm"), len(groups))
            v.tensor_copy(T["yT"][:, c, :], PS[6 + c][:, :]).then_inc(sem("y_out"), 1)
            v.tensor_copy(T["yT"][:, 4 + c, :], PS[4 + c][:, :]).then_inc(sem("y_out"), 1)
        dve.wait_ge(sem("pool_mm"), 1)
        for c in range(2):
            for b in range(2):
                pb = slice(HD * b, HD * b + HD)
                v.tensor_scalar(T["yT"][pb, 2 + c, :], PS[2 * c + b][pb, :], cols[pb, 64 + c:65 + c], None,
                                ALU.mult).then_inc(sem("y_out"), 1)

    def act_attention(act):
        a = nc.scalar
        act.wait_ge(sem("var"), 3)
        a.activation(rso, sso, ACT.Sqrt).then_inc(sem("sd"), 1)
        act.wait_ge(sem("hid_mm"), 1)
        for b, bank in enumerate((5, 6)):
            pb = slice(HD * b, HD * b + HD)
            a.activation(T["hid"][pb, 0:NCMP], PS[bank][pb, 0:NCMP], ACT.Silu).then_inc(sem("hid"), 1)
        act.wait_ge(sem("bc_in"), 80)
        act.wait_ge(sem("y_out"), 2)
        for u in range(NU + 3):
            if u < NU:
                gi, kind, h, i, j0, nk = units[u]
                act.wait_ge(sem("max"), u + 1)
                if u >= 2:
                    act.wait_ge(sem("prob_tr"), u - 1)
                m = nm[:, u % 2:u % 2 + 1]
                if kind == "swa":
                    a.activation(esk[:, u % 2:u % 2 + 1], sinkb[:, h:h + 1], ACT.Exp, bias=m)
                a.activation(T["pr"][:, u % 2, 0:nk], PS[u % 2][:, 0:nk], ACT.Exp, bias=m,
                             accum_out=den[:, u % 2:u % 2 + 1]).then_inc(sem("exp"), 1)
            if u >= 3:
                w = u - 3
                gi, kind, h, i, j0, nk = units[w]
                act.wait_ge(sem("prob_tr"), w + 1)
                if i == 0 and gi >= 2:
                    act.wait_ge(sem("pv_mm"), gi - 1)
                tok = slice(i * P, (i + 1) * P)
                if kind == "cmp":
                    ins = a.activation(T["pTr"][0:NCMP, gi % 2, 0, tok], PS[2 + w % 2][0:NCMP, 0:P], ACT.Copy)
                else:
                    nb = nk // P
                    ins = a.activation(T["pTr"][:, gi % 2, j0:j0 + nb, tok],
                                       PS[2 + w % 2][:, 0:nk].rearrange("p (j c) -> p j c", j=nb), ACT.Copy)
                ins.then_inc(sem("pT_out"), 1)

    def pool_compress(pool):
        g = nc.gpsimd
        all_out(pool, NI - 1)
        x = T["kcvT"][:, 0, :].rearrange("p (n l) -> p n l", l=CMP_STRIDE)
        for b in range(2):
            pos = cols[:, 91 + CMP_STRIDE * b:91 + CMP_STRIDE * (b + 1)]
            ins = g.tensor_tensor(T["kpos"][:, b, :].rearrange("p (n l) -> p n l", l=CMP_STRIDE), x,
                                  pos.unsqueeze(1).broadcast_to([P, S // CMP_STRIDE, CMP_STRIDE]), ALU.add)
        ins.then_inc(sem("kpos"), 1)

    def pool_windows(pool):
        g = nc.gpsimd
        link = pool_link[0]
        pool.wait_ge(sem("scan_end"), ST)
        pool.wait_ge(sem("scan_mm"), NCH)
        x, a, b, d = T["plT"], T["pa"], T["pb"], T["pd"]
        src, dst = x, a
        where = [(0, HD, 0), (HD, P, 0), (0, HD, 1), (HD, P, 1)]
        for n, w in enumerate(POOLW):
            s = w // 2
            for p0, p1, c in where[n:]:
                g.tensor_copy(dst[p0:p1, c, 0:s], src[p0:p1, c, 0:s])
                ins = g.tensor_tensor(dst[p0:p1, c, s:S], src[p0:p1, c, s:S], src[p0:p1, c, 0:S - s], ALU.add)
            link(ins)
            p0, p1, c = where[n]
            pool.wait_ge(sem("cnt"), 1)
            link(g.tensor_scalar(d[p0:p1, c, w:S], dst[p0:p1, c, w:S], 1.0 / w, 0.0, ALU.mult, ALU.add))
            link(g.tensor_tensor(d[p0:p1, c, 0:w], dst[p0:p1, c, 0:w], poolrec[p0:p1, 0:w], ALU.mult))
            ins = g.tensor_tensor(d[p0:p1, c, :], d[p0:p1, c, :], x[p0:p1, c, :], ALU.subtract)
            if n < 3:
                link(ins)
            else:
                ins.then_inc(sem("pool_d"), 1)
            src, dst = dst, (b if dst is a else a)
    xn2_d = nc.dram_tensor("xn2_rows", [S, D], F32).ap()
    list_d = nc.dram_tensor("slot_tokens", [ROWS, 1], U32).ap()
    yo_d = nc.dram_tensor("expert_rows", [ROWS, D], F32).ap()
    wg_v, wu_v = (A[n][0].rearrange("g e (k p) f -> (g e) p k f", p=P) for n in ("w_gate", "w_up"))
    wd_v = A["w_down"][0].rearrange("g e (k p) d -> (g e) p k d", p=P)
    gu, dn = (T["gu0"], T["gu1"]), (T["dn0"], T["dn1"])
    NPAIR = E // 2

    def load_gate_up(q, e, b):
        for n, v in enumerate((wg_v, wu_v)):
            q.dma_start(gu[b][:, n], v[e]).then_inc(sem(f"gu_in{b}"), 16)

    def load_down(q, e, b):
        q.dma_start(dn[b][:], wd_v[e]).then_inc(sem(f"dn_in{b}"), 16)

    def sync_moe(sp):
        sp.wait_ge(sem("ada_used"), HPS)
        load_gate_up(sp, 0, 0)
        sp.wait_ge(sem("scan_end"), ST)
        for i in range(ST):
            if i == 2:
                sp.wait_ge(sem("y_out"), 10)
                load_down(sp, 0, 0)
            if i >= 2:
                sp.wait_ge(sem("x2"), i - 1)
            sp.dma_start(T["xr"][:, i % 2], A["x"][0, i * P:(i + 1) * P, :]).then_inc(sem(f"xr_in{i % 2}"), 16)
        for i in range(ST):
            if i == 3:
                sp.wait_ge(sem("oproj_mm"), ST)
                load_gate_up(sp, 1, 1)
            sp.wait_ge(sem("xn2"), i + 1)
            sp.dma_start(xn2_d[i * P:(i + 1) * P, :], T["xn2"][:, i % 2, :]).then_inc(sem(f"xn2_st{i % 2}"), 16)
        sp.dma_start(T["fnb"][:], A["final_norm"].partition_broadcast(P)).then_inc(sem("fn_in"), 16)
        with sp.Fori(0, NPAIR - 1) as j:
            for b in range(2):
                sp.wait_ge(sem("gu_mm"), j * 2 + (b + 1))
                load_gate_up(sp, j * 2 + (b + 2), b)
        sp.wait_ge(sem("route_i"), 1)
        n_extra = sp.value_load(T["route_i"][0:1, 0:1], min_val=0, max_val=EXTRA)
        for x in range(EXTRA):
            with sp.If(n_extra > x):
                e = sp.value_load(T["route_i"][0:1, 1 + x:2 + x], min_val=0, max_val=E - 1)
                sp.wait_ge(sem("dn_mm"), E + x)
                load_gate_up(sp, e, 0)
                load_down(sp, e, 0)
        for i in range(ST):
            sp.wait_ge(sem("final"), i + 1)
            sp.dma_start(out[0, i * P:(i + 1) * P, :], T["x2"][:, i, :]).then_inc(sem("out_st"), 16)
        sp.wait_ge(sem("out_st"), 16 * ST)

    def pe_rows(pe, n, b, came):
        pe.wait_ge(sem(f"xg_in{b}"), came)
        pe.wait_ge(sem("xgT_a"), n)
        pe.wait_ge(sem("xgT_d"), n)
        for k in range(KT):
            ins = nc.tensor.transpose(PS[6 + k // 4][:, (k % 4) * P:(k % 4 + 1) * P],
                                      T["xg"][:, b, k * P:(k + 1) * P], idf[:])
        ins.then_inc(sem("xg_tr"), 1)

    def pe_gate_up(pe, n, b, came):
        pe.wait_ge(sem(f"gu_in{b}"), came)
        pe.wait_ge(sem("xgT_a"), n + 1)
        pe.wait_ge(sem("xgT_d"), n + 1)
        for k in range(KT):
            for w in range(2):
                ins = nc.tensor.matmul(PS[2 * b + w][:, :], T["xgT"][:, k, :], gu[b][:, w, k, :], start=(k == 0),
                                       stop=(k == KT - 1))
        ins.then_inc(sem("gu_mm"), 1)

    def pe_hidden(pe, n, b):
        pe.wait_ge(sem("hidm"), n + 1)
        for f in range(FT):
            ins = nc.tensor.transpose(PS[2 * b][:, f * P:(f + 1) * P], T["hidm"][:, f * P:(f + 1) * P], idf[:])
        ins.then_inc(sem("hid_tr"), 1)

    def pe_down(pe, n, b, came, first=False):
        pe.wait_ge(sem("hidT"), n + 1)
        pe.wait_ge(sem(f"dn_in{b}"), came)
        if not first:
            pe.wait_ge(sem("yo_a"), n)
            pe.wait_ge(sem("yo_d"), n)
        for f in range(FT):
            for w in range(2):
                ins = nc.tensor.matmul(PS[4 + w][:, :], T["hidT"][:, f, :], dn[b][:, f, w * 512:(w + 1) * 512],
                                       start=(f == 0), stop=(f == FT - 1))
        ins.then_inc(sem("dn_mm"), 1)

    def act_rows(act, n):
        act.wait_ge(sem("xg_tr"), n + 1)
        for k in range(4):
            ins = nc.scalar.activation(T["xgT"][:, k, :], PS[6][:, k * P:(k + 1) * P], ACT.Identity,
                                       scale=A2[:, k:k + 1], bias=mod[:, 24 + k:25 + k])
        ins.then_inc(sem("xgT_a"), 1)

    def act_silu(act, n, b):
        act.wait_ge(sem("gu_mm"), n + 1)
        nc.scalar.activation(T["sg"][:], PS[2 * b][:, :], ACT.Silu).then_inc(sem("sg"), 1)

    def act_hidden(act, n, b):
        act.wait_ge(sem("hid_tr"), n + 1)
        nc.scalar.activation(T["hidT"][:].rearrange("p a b -> p (a b)"), PS[2 * b][:, :],
                             ACT.Copy).then_inc(sem("hidT"), 1)

    def act_output(act, n, first=False):
        act.wait_ge(sem("dn_mm"), n + 1)
        if not first:
            act.wait_ge(sem("yo_st"), n * 16)
        nc.scalar.activation(T["yo"][:, 0:512], PS[4][:, :], ACT.Copy).then_inc(sem("yo_a"), 1)
        act.wait_ge(sem("yo_a"), n + 1)
        act.wait_ge(sem("yo_d"), n + 1)
        act.dma_start(yo_d.rearrange("(t p) d -> t p d", p=P)[n], T["yo"][:]).then_inc(sem("yo_st"), 16)

    def dve_rows(dve, n):
        dve.wait_ge(sem("xg_tr"), n + 1)
        for k in range(4, KT):
            ins = nc.vector.tensor_scalar(T["xgT"][:, k, :], PS[7][:, (k - 4) * P:(k - 3) * P], A2[:, k:k + 1],
                                          mod[:, 24 + k:25 + k], ALU.mult, ALU.add)
        ins.then_inc(sem("xgT_d"), 1)

    def dve_product(dve, n, b):
        dve.wait_ge(sem("sg"), n + 1)
        nc.vector.tensor_tensor(T["hidm"][:], T["sg"][:], PS[2 * b + 1][:, :], ALU.mult).then_inc(sem("hidm"), 1)

    def dve_output(dve, n, first=False):
        dve.wait_ge(sem("dn_mm"), n + 1)
        if not first:
            dve.wait_ge(sem("yo_st"), n * 16)
        nc.vector.tensor_copy(T["yo"][:, 512:D], PS[5][:, :]).then_inc(sem("yo_d"), 1)

    def extras(eng, body):
        eng.wait_ge(sem("route_i"), 1)
        n_extra = eng.value_load(T["route_i"][0:1, 0:1], min_val=0, max_val=EXTRA)
        for x in range(EXTRA):
            with eng.If(n_extra > x):
                body(x, E + x)

    def pe_moe(pe):
        t = nc.tensor
        pe.wait_ge(sem("wout_in"), 16)
        pe.wait_ge(sem("wr_in"), 64)
        pe.wait_ge(sem("y_out"), 10)
        for i in range(ST + 1):
            if i < ST:
                if i >= 2:
                    pe.wait_ge(sem("x2"), i - 1)
                for k in range(KT):
                    for n in range(2):
                        ins = t.matmul(PS[2 * (i % 2) + n][:, :], T["yT"][:, k, i * P:(i + 1) * P],
                                       T["wout"][:, k, n * 512:(n + 1) * 512], start=(k == 0), stop=(k == KT - 1))
                ins.then_inc(sem("oproj_mm"), 1)
            if i >= 1:
                w = i - 1
                pe.wait_ge(sem("xn2"), w + 1)
                if w:
                    pe.wait_ge(sem("x2T"), 2 * w)
                for k in range(KT):
                    ins = t.transpose(PS[4 + k // 4][:, (k % 4) * P:(k % 4 + 1) * P],
                                      T["xn2"][:, w % 2, k * P:(k + 1) * P], idf[:])
                ins.then_inc(sem("x2_tr"), 1)
                pe.wait_ge(sem("x2T"), 2 * w + 2)
                pe.wait_ge(sem("wrA"), 1)
                lg = PS[7][:, w * 20:w * 20 + 20]
                for k in range(KT):
                    t.matmul(lg, T["x2T"][:, k, :], T["wrA"][:, k, :], start=(k == 0), stop=False)
                    ins = t.matmul(lg, mod[:, 24 + k:25 + k].broadcast_to([P, P]), T["wr"][:, k, :], start=False,
                                   stop=(k == KT - 1))
                ins.then_inc(sem("logit_mm"), 1)
        pe.wait_ge(sem("chosen"), 1)
        ch = T["chosen"]
        for i in range(ST):
            o = PS[6][:, i * E:(i + 1) * E]
            for w in range(i):
                t.matmul(o, T["ones"][:], ch[:, w, :], start=(w == 0), stop=False)
            t.matmul(o, T["before"][:], ch[:, i, :], start=(i == 0), stop=True)
        for w in range(ST):
            ins = t.matmul(PS[6][:, ST * E:(ST + 1) * E], T["ones"][:], ch[:, w, :], start=(w == 0), stop=(w == ST - 1))
        ins.then_inc(sem("rank_mm"), 1)
        pe.wait_ge(sem("route_i"), 1)
        pe_rows_first(pe)
        pe_gate_up(pe, 0, 0, 32)
        pe_rows(pe, 1, 1, 16)
        with pe.Fori(0, NPAIR - 1) as j:
            for n, b in ((j * 2 + 1, 1), (j * 2 + 2, 0)):
                pe_hidden(pe, n - 1, 1 - b)
                pe_gate_up(pe, n, b, j * 32 + (32 if b else 64))
                pe_down(pe, n - 1, 1 - b, j * 16 + 16)
                pe_rows(pe, n + 1, 1 - b, j * 16 + 32)
        pe_hidden(pe, E - 2, 0)
        pe_gate_up(pe, E - 1, 1, 32 * NPAIR)
        pe_down(pe, E - 2, 0, 16 * NPAIR)
        pe_hidden(pe, E - 1, 1)
        pe_down(pe, E - 1, 1, 16 * NPAIR)

        def extra(x, n):
            pe_rows(pe, n, 0, 16 * (NPAIR + x + 1))
            pe_gate_up(pe, n, 0, 32 * (NPAIR + x + 1))
            pe_hidden(pe, n, 0)
            pe_down(pe, n, 0, 16 * (NPAIR + x + 1))

        extras(pe, extra)

    def pe_rows_first(pe):
        pe.wait_ge(sem("xg_in0"), 16)
        for k in range(KT):
            ins = nc.tensor.transpose(PS[6 + k // 4][:, (k % 4) * P:(k % 4 + 1) * P], T["xg"][:, 0, k * P:(k + 1) * P],
                                      idf[:])
        ins.then_inc(sem("xg_tr"), 1)

    def act_moe(act):
        a = nc.scalar
        for i in range(ST):
            act.wait_ge(sem("x2"), i + 1)
            if i:
                act.wait_ge(sem("ss"), ST + i)
            a.activation(T["sqs"][:], T["x2"][:, i, :], ACT.Square, accum_out=ss2[:, i:i + 1]).then_inc(sem("ss"), 1)
            act.wait_ge(sem("var"), 3 + i + 1)
            a.activation(rstd2[:, i:i + 1], ss2[:, i:i + 1], ACT.Sqrt).then_inc(sem("sd"), 1)
            act.wait_ge(sem("x2_tr"), i + 1)
            if i:
                act.wait_ge(sem("logit_mm"), i)
            for n in range(2):
                a.activation(T["x2T"][:, 4 * n:4 * n + 4, :].rearrange("p a b -> p (a b)"), PS[4 + n][:, :],
                             ACT.Copy).then_inc(sem("x2T"), 1)
        act.wait_ge(sem("exp_in"), 1)
        a.activation(T["eg"][:], T["eg"][:], ACT.Exp).then_inc(sem("exp_out"), 1)
        act.wait_ge(sem("exp_in"), 2)
        a.activation(T["ed"][:], T["ed"][:], ACT.Exp).then_inc(sem("exp_out"), 1)
        load_down(act, 1, 1)
        act_rows(act, 0)
        act_silu(act, 0, 0)
        act_rows(act, 1)
        with act.Fori(0, NPAIR - 1) as j:
            for n, b in ((j * 2 + 1, 1), (j * 2 + 2, 0)):
                act_hidden(act, n - 1, 1 - b)
                act_silu(act, n, b)
                act_output(act, n - 1)
                load_down(act, n + 1, 1 - b)
                act_rows(act, n + 1)
        act_hidden(act, E - 2, 0)
        act_silu(act, E - 1, 1)
        act_output(act, E - 2)
        act_hidden(act, E - 1, 1)
        act_output(act, E - 1)

        act.wait_ge(sem("yo_zero"), 16 * EXTRA)

        def extra(x, n):
            act_rows(act, n)
            act_silu(act, n, 0)
            act_hidden(act, n, 0)
            act_output(act, n)

        extras(act, extra)
        for i in range(ST):
            act.wait_ge(sem(f"y_in{i}"), 32)
            act.wait_ge(sem("w12"), 1)
            a.activation(T["y2"][:, i, :], T["y2"][:, i, :], ACT.Copy, scale=T["w2t"][:, i:i + 1]).then_inc(sem("y2w"), 1)
            act.wait_ge(sem("x3"), i + 1)
            if i:
                act.wait_ge(sem("ss"), 2 * ST + i)
            a.activation(T["sqs"][:], T["x2"][:, i, :], ACT.Square, accum_out=ss[:, i:i + 1]).then_inc(sem("ss"), 1)
            act.wait_ge(sem("var"), 3 + ST + i + 1)
            a.activation(rstd[:, i:i + 1], ss[:, i:i + 1], ACT.Sqrt).then_inc(sem("sd"), 1)

    def dve_moe(dve):
        v = nc.vector
        link = dve_link[0]
        dve.wait_ge(sem("wr_in"), 64)
        v.tensor_tensor(T["wrA"][:], T["wr"][:], A2.unsqueeze(2).broadcast_to([P, KT, 20]),
                        ALU.mult).then_inc(sem("wrA"), 1)
        dve.wait_ge(sem("gb"), 4)
        for i in range(ST):
            dve.wait_ge(sem("oproj_mm"), i + 1)
            dve.wait_ge(sem(f"xr_in{i % 2}"), 16 * (i // 2 + 1))
            for n in range(2):
                link(v.tensor_tensor(T["x2"][:, i, n * 512:(n + 1) * 512], PS[2 * (i % 2) + n][:, :],
                                     T["g1b"][:, n * 512:(n + 1) * 512], ALU.mult))
            v.tensor_tensor(T["x2"][:, i, :], T["x2"][:, i, :], T["xr"][:, i % 2], ALU.add).then_inc(sem("x2"), 1)
            c = slice(i, i + 1)
            dve.wait_ge(sem("ss"), ST + i + 1)
            v.tensor_scalar(ss2[:, c], ss2[:, c], 1.0 / D, EPS, ALU.mult, ALU.add).then_inc(sem("var"), 1)
            dve.wait_ge(sem("sd"), 3 + i + 1)
            link(v.reciprocal(rstd2[:, c], rstd2[:, c]))
            if i >= 2:
                dve.wait_ge(sem("x2_tr"), i - 1)
                dve.wait_ge(sem(f"xn2_st{i % 2}"), 16)
            v.tensor_scalar(T["xn2"][:, i % 2, :], T["x2"][:, i, :], rstd2[:, c], None, ALU.mult).then_inc(sem("xn2"), 1)
        dve.wait_ge(sem("logit_mm"), ST)
        dve.wait_ge(sem("cnt"), 1)
        lg = T["lg"]
        link(v.tensor_tensor(lg[:], PS[7][:, 0:ST * 20].rearrange("p (i e) -> p i e", i=ST),
                             T["rb"][:].unsqueeze(1).broadcast_to([P, ST, 20]), ALU.add))
        rg, mx, t4, mn, jm = lg[:, :, 0:G], T["mx"][:], T["t4"][:], T["mn"][:], T["jm"][:]

        def wide(x, n=4):
            return x.unsqueeze(2).broadcast_to([P, ST, n])

        def top(src, first):
            link(v.tensor_reduce(mx, src, AX.X, ALU.max))
            link(v.tensor_tensor(t4, src, wide(mx), ALU.is_equal))
            link(v.tensor_tensor(t4, t4, jm.unsqueeze(1).broadcast_to([P, ST, 4]), ALU.mult))
            link(v.tensor_reduce(mn, t4, AX.X, ALU.min))
            link(v.tensor_tensor(first, jm.unsqueeze(1).broadcast_to([P, ST, 4]), wide(mn), ALU.is_equal))

        ohg, oh1, oh2, le, m1 = (T[n][:] for n in ("ohg", "oh1", "oh2", "le", "m1"))
        top(rg, ohg)
        v.tensor_tensor(T["eg"][:], rg, wide(mx), ALU.subtract).then_inc(sem("exp_in"), 1)
        e16 = T["e16"]
        e4 = e16[:].rearrange("p i (g e) -> p i g e", g=G)
        link(v.tensor_tensor(e4, lg[:, :, G:20].rearrange("p i (g e) -> p i g e", g=G),
                             ohg.unsqueeze(3).broadcast_to([P, ST, G, EG]), ALU.mult))
        link(v.tensor_reduce(le, e16[:].rearrange("p i (g e) -> p i e g", g=G), AX.X, ALU.add))
        top(le, oh1)
        link(v.tensor_copy(m1, mx))
        link(v.scalar_tensor_tensor(le, oh1, NEG, le, ALU.mult, ALU.add))
        top(le, oh2)
        v.tensor_tensor(T["ed"][:], mx, m1, ALU.subtract).then_inc(sem("exp_in"), 1)
        for n, (o, oh) in enumerate((("M1", oh1), ("M2", oh2))):
            link(v.tensor_tensor(T[o][:].rearrange("p i (g e) -> p i g e", g=G),
                                 ohg.unsqueeze(3).broadcast_to([P, ST, G, EG]),
                                 oh.unsqueeze(2).broadcast_to([P, ST, G, EG]), ALU.mult))
        v.tensor_tensor(T["chosen"][:], T["M1"][:], T["M2"][:], ALU.add).then_inc(sem("chosen"), 1)
        w1, w2, ed = T["w1t"][:], T["w2t"][:], T["ed"][:]
        dve.wait_ge(sem("exp_out"), 1)
        link(v.tensor_reduce(w1, T["eg"][:], AX.X, ALU.add))
        dve.wait_ge(sem("exp_out"), 2)
        link(v.scalar_tensor_tensor(w1, ed, 1.0, w1, ALU.add, ALU.mult))
        link(v.reciprocal(w1, w1))
        v.tensor_tensor(w2, w1, ed, ALU.mult).then_inc(sem("w12"), 1)
        dve.wait_ge(sem("rank_mm"), 1)
        rank, cnt, xe, t16, incl, bb = (T[n][:] for n in ("rank", "count", "xe", "t16", "incl", "bb"))
        link(v.tensor_copy(rank, PS[6][:, 0:ST * E].rearrange("p (i e) -> p i e", i=ST)))
        link(v.tensor_copy(cnt, PS[6][:, ST * E:(ST + 1) * E]))
        link(v.tensor_scalar(xe, cnt, float(P), None, ALU.is_gt))
        for m in (2, 3):
            link(v.tensor_scalar(t16, cnt, float(m * P), None, ALU.is_gt))
            link(v.tensor_tensor(xe, xe, t16, ALU.add))
        link(v.memset(t16, 0.0))
        link(v.tensor_tensor_scan(incl, xe, t16, 0.0, ALU.add, ALU.add))
        link(v.tensor_tensor(bb, incl, xe, ALU.subtract))
        link(v.tensor_scalar(bb, bb, float(E - 1), float(P), ALU.add, ALU.mult))
        e128 = T["e128"][:]
        link(v.tensor_tensor(bb, bb, e128, ALU.subtract))
        link(v.tensor_scalar(e16[:], rank, float(P), None, ALU.is_ge))
        link(v.tensor_tensor(e16[:], e16[:], bb.unsqueeze(1).broadcast_to([P, ST, E]), ALU.mult))
        link(v.tensor_tensor(e16[:], e16[:], rank, ALU.add))
        link(v.tensor_tensor(e16[:], e16[:], e128.unsqueeze(1).broadcast_to([P, ST, E]), ALU.add))
        for n, m in enumerate(("M1", "M2")):
            link(v.tensor_tensor(T["s16"][:], e16[:], T[m][:], ALU.mult))
            link(v.tensor_reduce(T["slotf"][:, n, :], T["s16"][:], AX.X, ALU.add))
        v.tensor_copy(T["slot"][:], T["slotf"][:]).then_inc(sem("slots"), 1)
        link(v.tensor_copy(T["rf"][:, 0:1], incl[:, E - 1:E]))
        for x in range(EXTRA):
            link(v.tensor_scalar(t16, incl, float(x), None, ALU.is_le))
            link(v.tensor_reduce(T["rf"][:, 1 + x:2 + x], t16, AX.X, ALU.add))
        link(v.tensor_scalar(T["rf"][:, 1:8], T["rf"][:, 1:8], float(E - 1), None, ALU.min))
        v.tensor_copy(T["route_i"][:], T["rf"][:]).then_inc(sem("route_i"), 1)
        dve_rows(dve, 0)
        dve_product(dve, 0, 0)
        dve_rows(dve, 1)
        with dve.Fori(0, NPAIR - 1) as j:
            for n, b in ((j * 2 + 1, 1), (j * 2 + 2, 0)):
                dve_product(dve, n, b)
                dve_output(dve, n - 1)
                dve_rows(dve, n + 1)
        dve_product(dve, E - 1, 1)
        dve_output(dve, E - 2)
        dve_output(dve, E - 1)

        def extra(x, n):
            dve_rows(dve, n)
            dve_product(dve, n, 0)
            dve_output(dve, n)

        extras(dve, extra)
        dve.wait_ge(sem("fn_in"), 16)
        for i in range(ST):
            c = slice(i, i + 1)
            y, x = T["y1"][:, i, :], T["x2"][:, i, :]
            dve.wait_ge(sem("y2w"), i + 1)
            link(v.scalar_tensor_tensor(y, y, w1[:, c], T["y2"][:, i, :], ALU.mult, ALU.add))
            link(v.tensor_tensor(y, y, T["g2b"][:], ALU.mult))
            v.tensor_tensor(x, x, y, ALU.add).then_inc(sem("x3"), 1)
            dve.wait_ge(sem("ss"), 2 * ST + i + 1)
            v.tensor_scalar(ss[:, c], ss[:, c], 1.0 / D, EPS, ALU.mult, ALU.add).then_inc(sem("var"), 1)
            dve.wait_ge(sem("sd"), 3 + ST + i + 1)
            link(v.reciprocal(rstd[:, c], rstd[:, c]))
            v.scalar_tensor_tensor(x, x, rstd[:, c], T["fnb"][:], ALU.mult, ALU.mult).then_inc(sem("final"), 1)

    def pool_moe(pool):
        g = nc.gpsimd
        at = bass.IndirectOffsetOnAxis
        pool.wait_ge(sem("list_zero"), 16)
        pool.wait_ge(sem("slots"), 1)
        for i in range(ST):
            for n in range(2):
                g.indirect_dma_start(list_d, at(ap=T["slot"][:, n, i:i + 1], axis=0), T["tok"][:, i:i + 1],
                                     None).then_inc(sem("list_put"), 16)
        pool.wait_ge(sem("list_put"), 16 * 2 * ST)
        pool.dma_start(T["list"][:], list_d.rearrange("(t p) o -> p (t o)", p=P), allow_slow_non_contiguous=True).then_inc(sem("list_in"), 16)
        pool.wait_ge(sem("list_in"), 16)
        for b in range(2):
            pool.wait_ge(sem(f"xn2_st{b}"), 32)

        def gather(n):
            g.indirect_dma_start(T["xg"][:, n % 2 if n < E else 0, :], None, xn2_d,
                                 at(ap=T["list"][:, n:n + 1], axis=0)).then_inc(
                sem(f"xg_in{n % 2 if n < E else 0}"), 16)

        for n in range(E):
            if n >= 2:
                pool.wait_ge(sem("xg_tr"), n - 1)
            gather(n)

        def extra(x, n):
            pool.wait_ge(sem("xg_tr"), n)
            gather(n)
            pool.wait_ge(sem("yo_st"), 16 * (n + 1))

        pool.wait_ge(sem("yo_st"), 16 * E)
        extras(pool, extra)
        for i in range(ST):
            for n, y in enumerate(("y1", "y2")):
                g.indirect_dma_start(T[y][:, i, :], None, yo_d,
                                     at(ap=T["slot"][:, n, i:i + 1], axis=0)).then_inc(sem(f"y_in{i}"), 16)

    @block.sync
    def _(sp):
        def load_ada(n):
            if n >= 2:
                sp.wait_ge(sem("ada_used"), n - 1)
            sp.dma_start(T["ada"][:, n % 2], ada_v[:, :, n * 512:(n + 1) * 512]).then_inc(sem(f"ada_in{n % 2}"), 16)

        for n in range(2):
            load_ada(n)
        for n in range(2, 4):
            load_ada(n)
        for g, (a, b) in enumerate(WIN_GROUPS):
            moved = {0: "aq", OFF["ckv"]: "ckv"}.get(a)
            if moved:
                for f, to in MOVED[moved]:
                    f, to = a + HD * f, a + HD * to
                    sp.dma_start(W[:, :, to:to + HD], win_v[:, :, f:f + HD]).then_inc(sem(f"win_in{g}"), 16)
                if moved == "ckv":
                    sp.dma_start(W[:, :, a:a + P], win_v[:, :, a:a + P]).then_inc(sem(f"win_in{g}"), 16)
                a += IN_SIZES[moved]
            sp.dma_start(W[:, :, a:b], win_v[:, :, a:b]).then_inc(sem(f"win_in{g}"), 16)
        sp.wait_ge(sem("xT"), KT)
        for name, o in (("g1b", 2 * D), ("g2b", 5 * D)):
            sp.dma_start(T[name][:], A["b_ada"][0, o:o + D].partition_broadcast(P)).then_inc(sem("gb_in"), 16)
        for n in range(4, HPS):
            load_ada(n)
        sp.wait_ge(sem("proj_mm"), NI)
        w1v = A["cmp_w1"][0].rearrange("b (l d) e -> b d l e", d=HD)
        sp.dma_start(T["w1"][0:HD], w1v[0]).then_inc(sem("w1_in"), 16)
        sp.dma_start(T["w1"][HD:P], w1v[1]).then_inc(sem("w1_in"), 16)
        sp.dma_start(T["w2"][0:HD], A["cmp_w2"][0, 0]).then_inc(sem("w1_in"), 16)
        sp.dma_start(T["w2"][HD:P], A["cmp_w2"][0, 1]).then_inc(sem("w1_in"), 16)
        sp.wait_ge(sem("kc_out"), 2)
        sp.dma_start(T["wout"][:], A["w_out"][0].rearrange("(k p) n -> p k n", p=P)).then_inc(sem("wout_in"), 16)
        sync_moe(sp)

    @block.gpsimd
    def _(pool):
        link = pool_link[0] = Link(pool, sem("pool_step"))
        g = nc.gpsimd

        def select(t, pattern, base, cm, fill, op=ALU.is_ge):
            link(g.affine_select(out=t, in_=t, pattern=pattern, compare_op=op, fill=fill, base=base,
                                 channel_multiplier=cm))

        for t in (idf[:], idb[:]):
            link(g.memset(t, 0.0))
            select(t, [[-1, P]], 0, 1, 1.0, ALU.not_equal)
        link(g.memset(T["ones"][:], 1.0))
        g.memset(one, 1.0).then_inc(sem("ident"), 1)
        g.memset(tiny, 1e-6).then_inc(sem("ident"), 1)
        for t, v in ((T["negdiag"], 0.0), (T["negprev"], 0.0), (T["negcmp"], 0.0), (T["negdec"], 0.0),
                     (T["tri"], 1.0), (T["sl"], 1.0), (T["lev"], 1.0)):
            link(g.memset(t[:], v))
        select(T["negdiag"][:], [[-1, P]], 0, 1, NEG)
        select(T["negprev"][:], [[1, P]], -1, -1, NEG)
        for i in range(ST):
            select(T["negcmp"][:, i], [[0, 2], [-CMP_STRIDE, NCMP]], P * i - CMP_LEN + 1, 1, NEG)
        select(T["negdec"][:], [[0, H], [-1, P]], 0, 1, NEG)
        v = T["negdec"][:].rearrange("p h (b r) -> p h b r", b=2)
        select(v, [[0, H], [CH, 2], [0, CH]], CH - 1, -1, NEG)
        select(T["tri"][:], [[1, P]], 0, -1, 0.0)
        select(T["tri"][:].rearrange("p (b r) -> p b r", b=2), [[-CH, 2], [0, CH]], 0, 1, 0.0)
        select(T["sl"][:], [[-1, P]], -1, 1, 0.0)
        select(T["sl"][:].rearrange("p (b r) -> p b r", b=2), [[CH, 2], [0, CH]], CH - 1, -1, 0.0)
        for lv in range(6):
            s = 1 << lv
            nb = P // (2 * s)
            v = T["lev"][:, lv, :].rearrange("p (b h r) -> p b h r", h=2, r=s)
            select(v, [[-2 * s, nb], [0, 2], [0, s]], -s, 1, 0.0)
            select(v, [[2 * s, nb], [0, 2], [0, s]], 2 * s - 1, -1, 0.0)
            select(v, [[0, nb], [-1, 2], [0, s]], 0, 0, 0.0)
        link(g.memset(T["before"][:], 1.0))
        select(T["before"][:], [[1, P]], -1, -1, 0.0)
        link(g.iota(T["cnt_i"][:], pattern=[[1, 16]], base=1, channel_multiplier=0))
        link(g.iota(T["jm_i"][:], pattern=[[1, 4]], base=-16, channel_multiplier=0))
        link(g.iota(T["e128_i"][:], pattern=[[P, E]], base=0, channel_multiplier=0))
        g.iota(T["tok"][:], pattern=[[P, ST]], base=0, channel_multiplier=1).then_inc(sem("masks"), 1)
        link(g.tensor_copy(poolrec, T["cnt_i"][:]))
        link(g.tensor_copy(T["jm"][:], T["jm_i"][:]))
        link(g.tensor_copy(T["e128"][:], T["e128_i"][:]))
        link(g.memset(T["zlist"][:], 0))
        g.dma_start(list_d.rearrange("(p t) o -> p (t o)", p=P), T["zlist"][:]).then_inc(sem("list_zero"), 16)
        g.memset(T["state"][:], 0.0).then_inc(sem("masks"), 1)

        pool.wait_ge(sem("A1"), 1)
        for k in range(1, KT, 2):
            pool.wait_ge(sem("xT_out"), k + 1)
            g.tensor_scalar(T["hT"][:, k, :], T["hT"][:, k, :], A1[:, k:k + 1], mod[:, k:k + 1],
                            ALU.mult, ALU.add).then_inc(sem("hT_pool"), 1)

        link(g.memset(T["zero"][:], 0.0))
        for x in range(EXTRA):
            r = (E + x) * P
            g.dma_start(yo_d[r:r + P, :].rearrange("p (a b) -> p a b", b=P),
                        T["zero"][:].unsqueeze(1).broadcast_to([P, D // P, P])).then_inc(sem("yo_zero"), 16)
        pool.wait_ge(sem("proj_mm"), NI)
        pool_compress(pool)
        pool.wait_ge(sem("dtok_out"), 6)
        g.tensor_tensor(T["qd"][:], T["dtok"][:, :, 0:GW], T["dtok"][:, :, 0:GW], ALU.mult).then_inc(sem("qk_sq"), 1)
        g.tensor_tensor(T["kd"][:], T["dtok"][:, :, GW:2 * GW], T["dtok"][:, :, GW:2 * GW],
                        ALU.mult).then_inc(sem("qk_sq"), 1)
        pool.wait_ge(sem("d_scales"), 1)
        for i in range(ST):
            def scaled(dst, src, col):
                o = T[dst][:, i, :].rearrange("p (h d) -> p h d", h=H)
                x = T["dtok"][:, i, src * GW:(src + 1) * GW].rearrange("p (h d) -> p h d", h=H)
                return g.tensor_tensor(o, x, col.unsqueeze(2).broadcast_to([P, H, HD]), ALU.mult)
            if i == 0:
                pool.wait_ge(sem("sq_sum"), 2)
            scaled("kbe", 1, rkbe[:, i, :])
            scaled("kd", 1, rkd[:, i, :])
            scaled("vb", 2, beta[:, i, :]).then_inc(sem("d_tok_pool"), 1)
        for i in range(ST):
            if i >= 1:
                pool.wait_ge(sem("dec_mm"), i)
            g.tensor_tensor(T["asl"][:], T["sl"][:].unsqueeze(1).broadcast_to([P, H, P]),
                            ga[:, i, :].unsqueeze(2).broadcast_to([P, H, P]), ALU.mult).then_inc(sem("asl"), 1)
            for lv in range(6):
                pool.wait_ge(sem("low"), i + 1)
                if lv == 1:
                    pool.wait_ge(sem("tt"), 5 * i + 1)
                if lv >= 2:
                    pool.wait_ge(sem("y_mm"), 5 * i + lv - 1)
                elif i >= 1:
                    pool.wait_ge(sem("y_mm"), 5 * i)
                g.tensor_tensor(T["cc"][:], T["low"][:], T["lev"][:, lv].unsqueeze(1).broadcast_to([P, H, P]),
                                ALU.mult).then_inc(sem("cc"), 1)
        pool_windows(pool)
        pool_moe(pool)

    @block.scalar
    def _(act):
        link = Link(act, sem("act_step"))
        a = nc.scalar
        rows = T["small"]
        q = sem("small_in")
        act.dma_start(T["small"][0:48, :], A["b_ada"][0].rearrange("(r c) -> r c", c=P)).then_inc(q, 16)
        act.dma_start(T["small"][48:56, :], A["norm_mix"][0].rearrange("(r c) -> r c", c=P)).then_inc(q, 16)
        act.dma_start(T["small"][56:64, :], A["norm_ffn"][0].rearrange("(r c) -> r c", c=P)).then_inc(q, 16)
        act.dma_start(T["small"][64:66, :], A["pool_scale"][0].rearrange("(r c) -> r c", c=P)).then_inc(q, 16)
        act.dma_start(T["small"][66:90, :], A["conv_w"][0].rearrange("j (r c) -> (j r) c", c=P)).then_inc(q, 16)
        for b in range(2):
            act.dma_start(T["small"][90:91, HD * b:HD * b + HD], A["dn_norm"]).then_inc(q, 16)
            act.dma_start(T["small"][91:123, HD * b:HD * b + HD], A["cmp_pos"][0, b]).then_inc(q, 16)
        act.dma_start(cT, A["c"][0].rearrange("(p k) -> p k", k=KT)).then_inc(sem("c_in"), 16)
        act.dma_start(T["x"][:], A["x"][0].rearrange("(i p) d -> p i d", p=P)).then_inc(sem("x_in"), 16)
        for n, (t, name) in enumerate(((sinkb, "attn_sink"), (alogb, "a_log"), (dtb, "dt_bias"))):
            act.dma_start(t, A[name][0].partition_broadcast(P)).then_inc(sem("bc_in"), 16)
        for b in range(2):
            act.dma_start(T["wpool"][HD * b:HD * b + HD],
                          A["w_pool"][0].rearrange("(c b) i o -> b i c o", b=2)[b]).then_inc(sem("bc_in"), 16)
        act.dma_start(T["wr"][:, :, 0:G], A["w_route_group"][0].rearrange("(k p) e -> p k e", p=P)).then_inc(sem("wr_in"), 16)
        act.dma_start(T["wr"][:, :, G:20], A["w_route_expert"][0].rearrange("(k p) e -> p k e", p=P)).then_inc(sem("wr_in"), 16)
        act.dma_start(T["rb"][:, 0:G], A["b_route_group"][0].partition_broadcast(P)).then_inc(sem("wr_in"), 16)
        act.dma_start(T["rb"][:, G:20], A["b_route_expert"][0].partition_broadcast(P)).then_inc(sem("wr_in"), 16)
        act.wait_ge(sem("c_in"), 16)
        a.activation(csil, cT, ACT.Silu).then_inc(sem("csil"), 1)
        for i in range(ST):
            act.wait_ge(sem("x_in"), 16)
            if i:
                act.wait_ge(sem("ss"), i)
            a.activation(T["hT"][:, 0:2, :].rearrange("p a b -> p (a b)"), T["x"][:, i, :], ACT.Square,
                         accum_out=ss[:, i:i + 1]).then_inc(sem("ss"), 1)
        act.wait_ge(sem("var"), 1)
        a.activation(rstd, ss, ACT.Sqrt).then_inc(sem("sd"), 1)
        for k in range(0, KT, 2):
            act.wait_ge(sem("xT"), k + 1)
            if k:
                act.wait_ge(sem("xT_out"), k)
            a.activation(T["hT"][:, k, :], PS[k % 4][:, :], ACT.Copy).then_inc(sem("xT_out"), 1)
        def silu_conv(c):
            act.wait_ge(sem("conv_done"), c + 1)
            a.activation(T["cout"][:, c % 2, :], T["cout"][:, c % 2, :], ACT.Silu).then_inc(sem("conv_silu"), 1)

        for n in range(NI):
            if items[n][2] == "act":
                act.wait_ge(sem("proj_mm"), n + 1)
                empty_item(act, True, n)
            if 2 <= n < 8:
                silu_conv(n - 2)
        all_out(act, NI - 1)
        act.wait_ge(sem("bc_in"), 80)
        zb = T["zba"]
        a.activation(beta, zb[:, :, GW:GW + H], ACT.Sigmoid).then_inc(sem("scalars"), 1)
        a.activation(gate, T["cg"][:], ACT.Sigmoid).then_inc(sem("scalars"), 1)
        a.activation(zb[:, :, 0:GW], zb[:, :, 0:GW], ACT.Silu).then_inc(sem("scalars"), 1)
        a.activation(negA, alogb, ACT.Exp).then_inc(sem("scalars"), 1)
        act.wait_ge(sem("sp_abs"), 1)
        link(a.activation(sp2, sp2, ACT.Exp))
        act.wait_ge(sem("ident"), 2)
        a.activation(sp2, sp2, ACT.Ln, bias=one).then_inc(sem("sp_ln"), 1)
        act.wait_ge(sem("sq_sum"), 2)
        act.wait_ge(sem("var"), 2)
        a.activation(rqk, sqk, ACT.Sqrt).then_inc(sem("sd"), 1)
        act.wait_ge(sem("g_mm"), 1)
        a.activation(egc.rearrange("p a b -> p (a b)"), PS[6][:, 0:16], ACT.Exp)
        a.activation(kdec.rearrange("p a b -> p (a b)"), PS[6][:, 16:32], ACT.Exp)
        cv = cdec.rearrange("p (i f) h -> p f i h", f=2)
        for hf in range(2):
            ins = a.activation(cv[0:HD, hf], PS[6][0:HD, 32 + 16 * hf:48 + 16 * hf].rearrange("p (i h) -> p i h", i=ST),
                               ACT.Exp)
        ins.then_inc(sem("g_exp"), 1)
        for i in range(ST):
            act.wait_ge(sem("qk_tr"), i + 1)
            if i:
                act.wait_ge(sem("scan_mm"), NCH // ST * i)
            a.activation(T["qT"][:].rearrange("p a b -> p (a b)"), PS[0][0:HD, :], ACT.Copy)
            a.activation(T["qdT"][:].rearrange("p a b -> p (a b)"), PS[1][0:HD, :], ACT.Copy).then_inc(sem("qT_out"), 1)
            act.wait_ge(sem("dec_mm"), i + 1)
            a.activation(T["dec"][:].rearrange("p a b -> p (a b)"), PS[3][:, :], ACT.Exp).then_inc(sem("dec"), 1)
            act.wait_ge(sem("inT_tr"), i + 1)
            a.activation(T["inT"][:].rearrange("p a b -> p (a b)"), PS[0][:, :], ACT.Copy).then_inc(sem("inT_out"), 1)
            act.wait_ge(sem("uu_tr"), i + 1)
            a.activation(T["uu"][:].rearrange("p a b -> p (a b)"), PS[1][:, :], ACT.Copy).then_inc(sem("uu0"), 1)
            for lv in range(1, 6):
                act.wait_ge(sem("y_mm"), 5 * i + lv)
                a.activation(T["yy"][:].rearrange("p a b -> p (a b)"), PS[2][:, :], ACT.Copy).then_inc(sem("yy"), 1)
            act.wait_ge(sem("w_mm"), i + 1)
            a.activation(T["wT"][:].rearrange("p a b -> p (a b)"), PS[5][0:HD, :], ACT.Copy).then_inc(sem("wT_out"), 1)
            act.wait_ge(sem("scan_end"), i + 1)
            a.activation(T["osb"][:, i, :], PS[6][:, 0:GW], ACT.Copy).then_inc(sem("o_out"), 1)
        act_attention(act)
        act_moe(act)

    GB = {4: ("g1b", 0), 5: ("g1b", 1), 10: ("g2b", 0), 11: ("g2b", 1)}

    @block.vector
    def _(dve):
        v = nc.vector
        link = dve_link[0] = Link(dve, sem("dve_step"))
        dve.wait_ge(sem("small_tr"), 1)
        v.tensor_copy(cols[:, 0:123], PS[7][:, 0:123]).then_inc(sem("cols"), 1)
        dve.wait_ge(sem("ss"), ST)
        v.tensor_scalar(ss, ss, 1.0 / D, EPS, ALU.mult, ALU.add).then_inc(sem("var"), 1)
        dve.wait_ge(sem("sd"), 1)
        link(v.reciprocal(rstd, rstd))
        for i in range(ST):
            v.tensor_scalar(T["xn"][:, i, :], T["x"][:, i, :], rstd[:, i:i + 1], None, ALU.mult).then_inc(sem("xn"), 1)
        for k in range(1, KT, 2):
            dve.wait_ge(sem("xT"), k + 1)
            dve.wait_ge(sem("xT_out"), k)
            v.tensor_copy(T["hT"][:, k, :], PS[k % 4][:, :]).then_inc(sem("xT_out"), 1)
        dve.wait_ge(sem("ada_used"), 4)
        dve.wait_ge(sem("cols"), 1)
        link(v.tensor_tensor(mod[:, 0:16], PS[6][:, 0:16], cols[:, 0:16], ALU.add))
        v.scalar_tensor_tensor(A1, mod[:, 8:16], 1.0, cols[:, 48:56], ALU.add, ALU.mult).then_inc(sem("A1"), 1)
        dve.wait_ge(sem("A1"), 1)
        dve.wait_ge(sem("xT_out"), KT)
        for k in range(0, KT, 2):
            v.tensor_scalar(T["hT"][:, k, :], T["hT"][:, k, :], A1[:, k:k + 1], mod[:, k:k + 1],
                            ALU.mult, ALU.add).then_inc(sem("hT_dve"), 1)
        for b in range(2):
            dve.wait_ge(sem("xT"), KT)
            v.memset(T["cin"][:, b, 0:CONV], 0.0).then_inc(sem("cin_pad"), 1)

        def conv(c):
            dve.wait_ge(sem("proj_out_act"), c + 1)
            dve.wait_ge(sem("cin_pad"), 2)
            if c >= 2:
                dve.wait_ge(sem("conv_tr"), c - 1)
            x, y = T["cin"], T["cout"][:, c % 2, :]
            w = [cols[:, 66 + 6 * j + c:67 + 6 * j + c] for j in range(CONV)]
            link(v.tensor_scalar(y, x[:, c % 2, CONV:CONV + S], w[3], None, ALU.mult))
            for j in range(CONV - 1):
                ins = v.scalar_tensor_tensor(y, x[:, c % 2, 1 + j:1 + j + S], w[j], y, ALU.mult, ALU.add)
                if j < CONV - 2:
                    link(ins)
            ins.then_inc(sem("conv_done"), 1)

        for n in range(NI):
            if items[n][2] == "dve":
                dve.wait_ge(sem("proj_mm"), n + 1)
                empty_item(dve, False, n)
            if n < 6:
                conv(n)
            if 3 <= n < 9:
                c = n - 3
                dve.wait_ge(sem("conv_tr"), c + 1)
                v.tensor_copy(T["dtok"][:, :, c * P:(c + 1) * P],
                              PS[6 + c % 2][:, :].rearrange("p (i c) -> p i c", i=ST)).then_inc(sem("dtok_out"), 1)
            if 11 <= n < 19 and n - 11 + 4 in GB:
                hp = n - 11 + 4
                name, half = GB[hp]
                dve.wait_ge(sem("ada_used"), hp + 1)
                dve.wait_ge(sem("gb_in"), 32)
                o = T[name][:, half * 512:(half + 1) * 512]
                v.tensor_tensor(o, PS[7][:, :], o, ALU.add).then_inc(sem("gb"), 1)
        dve.wait_ge(sem("ada_used"), 10)
        link(v.tensor_tensor(mod[:, 24:40], PS[6][:, 24:40], cols[:, 24:40], ALU.add))
        link(v.scalar_tensor_tensor(A2, mod[:, 32:40], 1.0, cols[:, 56:64], ALU.add, ALU.mult))
        all_out(dve, NI - 1)
        dve.wait_ge(sem("bc_in"), 80)
        za = T["zba"][:, :, GW + H:GW + 2 * H]
        link(v.tensor_tensor(sp1, za, dtb.unsqueeze(1).broadcast_to([P, ST, H]), ALU.add))
        v.scalar_tensor_tensor(sp2, sp1, -1.0, sp1, ALU.mult, ALU.min).then_inc(sem("sp_abs"), 1)
        dve.wait_ge(sem("sp_ln"), 1)
        link(v.scalar_tensor_tensor(sp1, sp1, 0.0, sp2, ALU.max, ALU.add))
        dve.wait_ge(sem("scalars"), 4)
        v.scalar_tensor_tensor(ga, sp1, -1.0, negA.unsqueeze(1).broadcast_to([P, ST, H]), ALU.mult,
                               ALU.mult).then_inc(sem("ga"), 1)
        dve.wait_ge(sem("qk_sq"), 2)
        for n, t in enumerate(("qd", "kd")):
            v.tensor_reduce(sqk[:, :, 4 * n:4 * n + 4], T[t][:].rearrange("p i (h d) -> p i h d", h=H),
                            AX.X, ALU.add).then_inc(sem("sq_sum"), 1)
        dve.wait_ge(sem("sq_sum"), 2)
        v.tensor_scalar(sqk, sqk, 1e-6, None, ALU.add).then_inc(sem("var"), 1)
        dve.wait_ge(sem("sd"), 2)
        link(v.reciprocal(rqk, rqk))
        rq, rk = rqk[:, :, 0:4], rqk[:, :, 4:8]
        link(v.tensor_scalar(rq, rq, 0.125, None, ALU.mult))
        dve.wait_ge(sem("g_exp"), 1)
        dve.wait_ge(sem("scalars"), 1)
        link(v.tensor_tensor(rqe, rq, egc, ALU.mult))
        link(v.tensor_tensor(rkd, rk, kdec, ALU.mult))
        link(v.tensor_tensor(rkbe, rk, egc, ALU.mult))
        v.tensor_tensor(rkbe, rkbe, beta, ALU.mult).then_inc(sem("d_scales"), 1)
        for i in range(ST):
            for n, (dst, src, col) in enumerate((("qn", 0, rq), ("qd", 0, rqe), ("kn", 1, rk))):
                o = T[dst][:, i, :].rearrange("p (h d) -> p h d", h=H)
                x = T["dtok"][:, i, src * GW:(src + 1) * GW].rearrange("p (h d) -> p h d", h=H)
                ins = v.tensor_tensor(o, x, col[:, i, :].unsqueeze(2).broadcast_to([P, H, HD]), ALU.mult)
            ins.then_inc(sem("d_tok_dve"), 1)
        low, tt, uu, yy = (T[n] for n in ("low", "tt", "uu", "yy"))

        def flat(t):
            return t[:].rearrange("p a b -> p (a b)")

        for i in range(ST):
            dve.wait_ge(sem("qk_tr"), i + 1)
            if i:
                dve.wait_ge(sem("kk_mm"), i)
            v.tensor_copy(flat(T["kT"]), PS[2][0:HD, :]).then_inc(sem("kT_out"), 1)
            dve.wait_ge(sem("dec"), i + 1)
            dve.wait_ge(sem("kk_mm"), i + 1)
            for h in range(H):
                ins = v.scalar_tensor_tensor(low[:, h, :], PS[4][:, h * P:(h + 1) * P], beta[:, i, h:h + 1],
                                             T["dec"][:, h, :], ALU.mult, ALU.mult)
            ins.then_inc(sem("low"), 1)
            dve.wait_ge(sem("low"), i + 1)
            v.tensor_tensor(flat(T["dec"]), PS[5][:, :], flat(T["dec"]), ALU.mult).then_inc(sem("intra"), 1)
            dve.wait_ge(sem("cc"), 6 * i + 1)
            link(v.tensor_scalar(flat(tt), flat(T["cc"]), -1.0, None, ALU.mult))
            v.tensor_tensor(tt[:], tt[:], idf[:].unsqueeze(1).broadcast_to([P, H, P]), ALU.add).then_inc(sem("tt"), 1)
            for lv in range(1, 6):
                dve.wait_ge(sem("du_mm"), 5 * i + lv)
                if lv < 5:
                    v.tensor_tensor(flat(tt), flat(tt), PS[3][:, :], ALU.subtract).then_inc(sem("tt"), 1)
                v.tensor_tensor(flat(uu), flat(uu), PS[4][:, :], ALU.subtract).then_inc(sem("uu"), 1)
            dve.wait_ge(sem("w_mm"), i + 1)
            if i:
                dve.wait_ge(sem("scan_mm"), 2 * i)
            v.tensor_copy(T["u"][:], PS[6][:, 0:GW]).then_inc(sem("u_out"), 1)
            dve.wait_ge(sem("u_out"), i + 1)
            link(v.tensor_copy(T["vnew"][:], T["u"][:]))
            for hf in range(2):
                c = 2 * i + hf
                pb = slice(CH * hf, CH * hf + CH)
                if c == 0:
                    v.tensor_copy(T["vnew"][pb], T["u"][pb]).then_inc(sem("vnew"), 1)
                else:
                    dve.wait_ge(sem("vn_mm"), c)
                    v.tensor_tensor(T["vnew"][pb], T["u"][pb], PS[7][pb, 0:GW], ALU.subtract).then_inc(sem("vnew"), 1)
                if c < NCH - 1:
                    st = T["state"][:].rearrange("p (h d) -> p h d", h=H)
                    dve.wait_ge(sem("scan_mm"), c + 1)
                    link(v.tensor_tensor(st, st, cdec[0:HD, c, :].unsqueeze(2).broadcast_to([HD, H, HD]), ALU.mult))
                    v.tensor_tensor(T["state"][:], T["state"][:], PS[7][0:HD, GW:2 * GW], ALU.add).then_inc(sem("state"), 1)
        for i in range(ST):
            dve.wait_ge(sem("o_out"), i + 1)
            link(v.tensor_tensor(T["qd"][:, i, :], T["osb"][:, i, :], T["osb"][:, i, :], ALU.mult))
        link(v.tensor_reduce(sso, T["qd"][:].rearrange("p i (h d) -> p i h d", h=H), AX.X, ALU.add))
        v.tensor_scalar(sso, sso, 1.0 / HD, EPS, ALU.mult, ALU.add).then_inc(sem("var"), 1)
        dve.wait_ge(sem("scalars"), 3)
        for i in range(ST):
            link(v.tensor_tensor(T["osb"][:, i, :], T["osb"][:, i, :], T["zba"][:, i, 0:GW], ALU.mult))
        dve.wait_ge(sem("sd"), 3)
        link(v.reciprocal(rso, rso))
        for i in range(ST):
            o = T["osb"][:, i, :].rearrange("p (h d) -> p h d", h=H)
            v.tensor_tensor(o, o, rso[:, i, :].unsqueeze(2).broadcast_to([P, H, HD]), ALU.mult).then_inc(sem("o_tok"), 1)
        for c in range(2):
            dve.wait_ge(sem("o_tr"), c + 1)
            v.tensor_scalar(T["yT"][:, 6 + c, :], PS[c][:, :], cols[:, 90:91], None, ALU.mult).then_inc(sem("y_out"), 1)
        dve_attention(dve)
        dve_moe(dve)

    @block.tensor
    def _(pe):
        t = nc.tensor
        pe.wait_ge(sem("ident"), 2)
        pe.wait_ge(sem("small_in"), 16 * 9)
        t.transpose(PS[7][:, 0:123], T["small"][0:123, :], idf[0:123, 0:123]).then_inc(sem("small_tr"), 1)
        for k in range(KT):
            pe.wait_ge(sem("xn"), ST)
            if k >= 4:
                pe.wait_ge(sem("xT_out"), k - 3)
            for i in range(ST):
                ins = t.transpose(PS[k % 4][:, i * P:(i + 1) * P], T["xn"][:, i, k * P:(k + 1) * P], idf[:])
            ins.then_inc(sem("xT"), 1)

        def ada(hp):
            pe.wait_ge(sem(f"ada_in{hp % 2}"), 16 * (hp // 2 + 1))
            if hp in GB:
                if hp > 4:
                    pe.wait_ge(sem("gb"), {5: 1, 10: 2, 11: 3}[hp])
                for k in range(KT):
                    ins = t.matmul(PS[7][:, :], csil[:, k:k + 1].broadcast_to([P, P]), T["ada"][:, hp % 2, k, :],
                                   start=(k == 0), stop=(k == KT - 1))
            else:
                for c in range(HP_CHUNKS):
                    for k in range(KT):
                        ins = t.matmul(PS[6][:, 4 * hp + c:4 * hp + c + 1], T["ada"][:, hp % 2, k, c * P:(c + 1) * P],
                                       csil[:, k:k + 1], start=(k == 0), stop=(k == KT - 1))
            ins.then_inc(sem("ada_used"), 1)

        pe.wait_ge(sem("csil"), 1)
        for hp in range(4):
            ada(hp)
        for n, (name, j, _) in enumerate(items):
            pe.wait_ge(sem(f"win_in{GROUP_OF[name]}"), 16 * GROUP_DMAS[GROUP_OF[name]])
            if n == 0:
                pe.wait_ge(sem("hT_dve"), KT // 2)
                pe.wait_ge(sem("hT_pool"), KT // 2)
            if n >= PB:
                bank_empty(pe, n - PB)
            bank = PS[n % PB]
            if name in ("zba", "v"):
                tok = slice(j * P, (j + 1) * P)
                if name == "zba":
                    cuts = [(bank[:, 0:ZBA], lambda k: W[:, k, OFF["dz"]:OFF["dz"] + ZBA])]
                else:
                    cuts = [(bank[:, 0:P], in_cols("av")), (bank[:, P:2 * P], in_cols("ckv", 4 * HD)),
                            (bank[:, 2 * P:2 * P + 12], in_cols("cg", 0, 12))]
                for o, w in cuts:
                    for k in range(KT):
                        ins = t.matmul(o, T["hT"][:, k, tok], w(k), start=(k == 0), stop=(k == KT - 1))
            else:
                w = {"cin": in_cols("dqkv", P * j), "kcvT": in_cols("ckv"), "ksw": in_cols("ckv", 2 * HD),
                     "cqT": in_cols("cq", P * j), "aqT": in_cols("aq", P * j), "akT": in_cols("ak"),
                     "plT": in_cols("pool", P * j)}[name]
                for k in range(KT):
                    ins = t.matmul(bank[:, :], w(k), T["hT"][:, k, :], start=(k == 0), stop=(k == KT - 1))
            ins.then_inc(sem("proj_mm"), 1)
            if 3 <= n < 9:
                c = n - 3
                pe.wait_ge(sem("conv_silu"), c + 1)
                if c >= 2:
                    pe.wait_ge(sem("dtok_out"), c - 1)
                for i in range(ST):
                    ins = t.transpose(PS[6 + c % 2][:, i * P:(i + 1) * P], T["cout"][:, c % 2, i * P:(i + 1) * P], idf[:])
                ins.then_inc(sem("conv_tr"), 1)
            if 10 <= n < 18:
                if n == 10:
                    pe.wait_ge(sem("dtok_out"), 6)
                ada(n - 10 + 4)
        pe.wait_ge(sem("ga"), 1)
        pe.wait_ge(sem("masks"), 2)
        gf = ga.rearrange("p a b -> p (a b)")
        t.matmul(PS[6][:, 0:16], T["tri"][:], gf, start=True, stop=True)
        t.matmul(PS[6][:, 16:32], T["sl"][:], gf, start=True, stop=True)
        for hf in range(2):
            ins = t.matmul(PS[6][0:HD, 32 + 16 * hf:48 + 16 * hf],
                           T["tri"][:, CH * hf + CH - 1:CH * hf + CH].broadcast_to([P, HD]), gf, start=True, stop=True)
        ins.then_inc(sem("g_mm"), 1)
        tt, uu, yy, cc = T["tt"], T["uu"], T["yy"], T["cc"]
        blk = [slice(h * P, (h + 1) * P) for h in range(H)]
        for i in range(ST):
            pe.wait_ge(sem("d_tok_dve"), i + 1)
            if i:
                pe.wait_ge(sem("qT_out"), i)
                pe.wait_ge(sem("kT_out"), i)
                pe.wait_ge(sem("inT_out"), i)
                pe.wait_ge(sem("uu"), 5 * i)
            for n, name in enumerate(("qn", "qd", "kn")):
                for h in range(H):
                    ins = t.transpose(PS[n][0:HD, blk[h]], T[name][:, i, h * HD:(h + 1) * HD], idf[:])
            ins.then_inc(sem("qk_tr"), 1)
            pe.wait_ge(sem("asl"), i + 1)
            t.matmul(PS[3][:, :], T["tri"][:], T["asl"][:].rearrange("p a b -> p (a b)"), start=True, stop=False)
            t.matmul(PS[3][:, :], idb[:], T["negdec"][:].rearrange("p a b -> p (a b)"), start=False,
                     stop=True).then_inc(sem("dec_mm"), 1)
            pe.wait_ge(sem("qT_out"), i + 1)
            pe.wait_ge(sem("kT_out"), i + 1)
            for h in range(H):
                t.matmul(PS[4][:, blk[h]], T["kT"][:, h, :], T["kT"][:, h, :], start=True, stop=True)
            for h in range(H):
                ins = t.matmul(PS[5][:, blk[h]], T["qT"][:, h, :], T["kT"][:, h, :], start=True, stop=True)
            ins.then_inc(sem("kk_mm"), 1)
            pe.wait_ge(sem("intra"), i + 1)
            for h in range(H):
                ins = t.transpose(PS[0][:, blk[h]], T["dec"][:, h, :], idf[:])
            ins.then_inc(sem("inT_tr"), 1)
            pe.wait_ge(sem("tt"), 5 * i + 1)
            for h in range(H):
                ins = t.transpose(PS[1][:, blk[h]], tt[:, h, :], idf[:])
            ins.then_inc(sem("uu_tr"), 1)
            for lv in range(1, 6):
                pe.wait_ge(sem("cc"), 6 * i + lv + 1)
                if lv == 1:
                    pe.wait_ge(sem("uu0"), i + 1)
                else:
                    pe.wait_ge(sem("uu"), 5 * i + lv - 1)
                for h in range(H):
                    ins = t.matmul(PS[2][:, blk[h]], cc[:, h, :], uu[:, h, :], start=True, stop=True)
                ins.then_inc(sem("y_mm"), 1)
                pe.wait_ge(sem("yy"), 5 * i + lv)
                pe.wait_ge(sem("tt"), 5 * i + lv)
                if lv < 5:
                    for h in range(H):
                        t.matmul(PS[3][:, blk[h]], yy[:, h, :], tt[:, h, :], start=True, stop=True)
                for h in range(H):
                    ins = t.matmul(PS[4][:, blk[h]], tt[:, h, :], yy[:, h, :], start=True, stop=True)
                ins.then_inc(sem("du_mm"), 1)
            pe.wait_ge(sem("uu"), 5 * i + 5)
            pe.wait_ge(sem("d_tok_pool"), i + 1)
            if i:
                pe.wait_ge(sem("o_out"), i)
            for h in range(H):
                t.matmul(PS[5][0:HD, blk[h]], T["kbe"][:, i, h * HD:(h + 1) * HD], uu[:, h, :], start=True, stop=True)
            for h in range(H):
                ins = t.matmul(PS[6][:, h * HD:(h + 1) * HD], uu[:, h, :], T["vb"][:, i, h * HD:(h + 1) * HD],
                               start=True, stop=True)
            ins.then_inc(sem("w_mm"), 1)
            pe.wait_ge(sem("wT_out"), i + 1)
            pe.wait_ge(sem("u_out"), i + 1)
            pe.wait_ge(sem("inT_out"), i + 1)
            for hf in range(2):
                c = 2 * i + hf
                pb = slice(CH * hf, CH * hf + CH)
                hd = [slice(h * HD, (h + 1) * HD) for h in range(H)]
                if c:
                    pe.wait_ge(sem("state"), c)
                    for h in range(H):
                        ins = t.matmul(PS[7][pb, hd[h]], T["wT"][:, h, pb], T["state"][:, hd[h]], start=True, stop=True)
                    ins.then_inc(sem("vn_mm"), 1)
                pe.wait_ge(sem("vnew"), c + 1)
                for h in range(H):
                    t.matmul(PS[6][pb, hd[h]], T["qdT"][:, h, pb], T["state"][:, hd[h]], start=True, stop=False)
                    ins = t.matmul(PS[6][pb, hd[h]], T["inT"][:, h, pb], T["vnew"][:, hd[h]], start=False, stop=True)
                if hf:
                    ins.then_inc(sem("scan_end"), 1)
                for h in range(H):
                    ins = t.matmul(PS[7][0:HD, GW + h * HD:GW + (h + 1) * HD], T["kd"][pb, i, hd[h]],
                                   T["vnew"][pb, hd[h]], start=True, stop=True)
                ins.then_inc(sem("scan_mm"), 1)
        for i in range(ST):
            pe.wait_ge(sem("o_tok"), i + 1)
        for c in range(2):
            for i in range(ST):
                ins = t.transpose(PS[c][:, i * P:(i + 1) * P], T["osb"][:, i, c * P:(c + 1) * P], idf[:])
            ins.then_inc(sem("o_tr"), 1)
        pe_attention(pe)
        pe_moe(pe)
    ctx.close()


_NAMES = ["x", "c", "norm_mix", "norm_ffn", "final_norm", "w_ada", "b_ada", "w_in", "w_out", "attn_sink", "w_pool",
          "pool_scale", "cmp_pos", "cmp_w1", "cmp_w2", "conv_w", "a_log", "dt_bias", "dn_norm", "w_route_group",
          "b_route_group", "w_route_expert", "b_route_expert", "w_gate", "w_up", "w_down"]


def kernel(**inputs):
    import numpy as np
    import concourse.bacc as bacc
    from concourse.bass_utils import run_bass_kernel_spmd

    nc = bacc.Bacc("TRN2", target_bir_lowering=False, num_devices=1)
    arrays, views = {}, {}
    for name in _NAMES:
        a = np.ascontiguousarray(inputs[name])
        arrays["in_" + name] = a
        views[name] = nc.dram_tensor("in_" + name, a.shape, mybir.dt.from_np(a.dtype), kind="ExternalInput").ap()
    out = nc.dram_tensor("out_y", (1, S, D), F32, kind="ExternalOutput").ap()
    build(nc, views, out)
    r = run_bass_kernel_spmd(nc, [arrays], core_ids=[0])
    return r.results[0]["out_y"]
```

```python
from contextlib import ExitStack

import concourse.bass as bass
from concourse import mybir

F32 = mybir.dt.float32
BF16 = mybir.dt.bfloat16
I32 = mybir.dt.int32
U32 = mybir.dt.uint32
ALU = mybir.AluOpType
ACT = mybir.ActivationFunctionType
AX = mybir.AxisListType

P = 128
D = 1024
KT = D // P
S = 512
ST = S // P
HD = 64
H = 4
GW = 256
IN_SIZES = dict(aq=256, ak=128, av=128, pool=256, cq=256, ckv=384, cg=12, dqkv=768, dz=256, db=4, da=4)
OFF = {}
_o = 0
for _n, _w in IN_SIZES.items():
    OFF[_n] = _o
    _o += _w
IN_W = _o
CONV = 4
POOLW = (2, 4, 8, 16)
CMP_LEN, CMP_STRIDE = 32, 16
NCMP = (S - CMP_LEN) // CMP_STRIDE + 1
CH = 64
NCH = S // CH
G, EG = 4, 4
E = G * EG
F = 512
FT = F // P
EXTRA = 7
ROWS = (E + EXTRA) * P
EPS = 1e-6
NEG = -1e30
ZBA = 256 + 8


class Link:

    def __init__(self, eng, done):
        self.eng, self.done, self.n = eng, done, 0

    def __call__(self, ins):
        self.n += 1
        ins.then_inc(self.done, 1)
        self.eng.wait_ge(self.done, self.n)


def sbuf_map(nc):
    base = 16512
    tensors = {}

    def at(name, off, shape, dt=F32):
        n = 4 if dt in (F32, I32, U32) else 2
        for x in shape[1:]:
            n *= x
        assert base + off + n <= 229368, (name, off, n)
        tensors[name] = nc.alloc_sbuf_tensor_at(name, shape, dt, offset=base + off)
        return off + (n + 31) // 32 * 32

    K = 1024
    R0 = 0
    at("ada", R0, [P, 2, KT, 512])
    at("gu0", R0, [P, 2, KT, F])
    R1 = 32 * K
    at("win", R1, [P, KT, IN_W])
    at("acc0", R1 + 77 * K, [P, 512])
    at("gu1", R1, [P, 2, KT, F])
    at("dn0", R1 + 32 * K, [P, FT, D])
    at("dn1", R1 + 48 * K, [P, FT, D])
    at("w1", R1, [P, CMP_LEN, HD])
    o = at("kpos", R1 + 8 * K, [P, 2, S])
    o = at("w2", o, [P, HD])
    o = at("hid", o, [P, 32])
    at("wout", R1, [P, KT, D])
    o = R1 + 32 * K
    for n in ("qn", "qd", "kn", "kbe", "kd", "vb"):
        o = at(n, o, [P, ST, GW])
    for n in ("qT", "qdT", "kT", "wT"):
        o = at(n, o, [HD, H, P])
    for n in ("asl", "dec", "low", "tt", "uu", "cc", "yy", "inT"):
        o = at(n, o, [P, H, P])
    assert o <= R1 + 80 * K
    at("cc1", R0 + 28 * K, [P, H, P])
    at("pTr", R0, [P, 2, ST, S])
    at("pa", R0 + 16 * K, [P, 2, S])
    at("pb", R0 + 20 * K, [P, 2, S])
    at("pd", R0 + 24 * K, [P, 2, S])
    at("osb", R1 + 32 * K, [P, ST, GW])
    at("x2", R1 + 64 * K, [P, ST, D])
    at("y1", R1, [P, ST, D])
    at("y2", R1 + 16 * K, [P, ST, D])
    RX = R1 + 80 * K
    at("x", RX, [P, ST, D])
    at("dtok", RX, [P, ST, 3 * GW])
    at("xr", R1 + 48 * K, [P, ST, D])
    at("sqs", RX + 8 * K, [P, D])
    at("g2b", RX + 12 * K, [P, D])
    RN = RX + 16 * K
    at("xn", RN, [P, ST, D])
    o = at("cin", RN, [P, 2, S + CONV])
    o = at("cout", o, [P, 2, S])
    at("sq", RN, [P, 2, ST, GW])
    at("pr", RN, [P, 2, S])
    at("xn2", RN, [P, 2, D])
    at("x2T", RN + 8 * K, [P, KT, P])
    at("fnb", RN + 12 * K, [P, D])
    at("g1b", RN + 12 * K, [P, D])
    RH = RN + 16 * K
    at("hT", RH, [P, KT, S])
    at("yT", RH, [P, KT, S])
    o = at("hidm", RH, [P, F])
    o = at("hidT", o, [P, FT, P])
    o = at("yo", o, [P, D])
    o = at("sg", o, [P, F])
    o = RH + 16 * K
    at("ada2", o, [P, KT, 512])
    o2 = at("xg", o, [P, 2, D])
    o2 = at("xgT", o2, [P, KT, P])
    for n, shape in (("lg", [P, ST, 20]), ("mx", [P, ST]), ("mn", [P, ST]), ("m1", [P, ST]), ("ed", [P, ST]),
                     ("t4", [P, ST, 4]), ("eg", [P, ST, 4]), ("ohg", [P, ST, 4]), ("oh1", [P, ST, 4]),
                     ("oh2", [P, ST, 4]), ("le", [P, ST, 4]), ("e16", [P, ST, E]), ("s16", [P, ST, E]),
                     ("M1", [P, ST, E]), ("M2", [P, ST, E]), ("chosen", [P, ST + 1, E]), ("rank", [P, ST, E]),
                     ("count", [P, E]), ("xe", [P, E]), ("t16", [P, E]), ("incl", [P, E]), ("bb", [P, E]),
                     ("w1t", [P, ST]), ("w2t", [P, ST]), ("slotf", [P, 2, ST]), ("rf", [P, 8])):
        o2 = at(n, o2, shape)
    o2 = at("place", o2, [P, 2, ST])
    o2 = at("first", o2, [P, 2, ST])
    o2 = at("r16", o2, [P, ST, E])
    o2 = at("in_row", o2, [P, 2, ST, P])
    o2 = at("in_tile", o2, [P, 2, ST, E + EXTRA])
    o2 = at("slot", o2, [P, 2, ST], U32)
    o2 = at("route_i", o2, [P, 8], I32)
    o2 = at("list", o2, [P, E + EXTRA], U32)
    for n, w in (("aqT", 2), ("akT", 1), ("plT", 2), ("cqT", 2), ("kcvT", 1), ("kselT", 1), ("kwinT", 1)):
        o = at(n, o, [P, w, S])
    o = at("va", o, [P, ST, P])
    o = at("vsw", o, [P, ST, P])
    o = at("cg", o, [P, ST, 12])
    o = at("zba", o, [P, ST, ZBA])
    o = at("idf", o, [P, P])
    o = at("idb", o, [P, P], BF16)
    o = at("negdiag", o, [P, P], BF16)
    o = at("negprev", o, [P, P], BF16)
    o = at("negcmp", o, [P, ST, 2, NCMP], BF16)
    o = at("negdec", o, [P, H, P], BF16)
    o = at("tri", o, [P, P])
    o = at("sl", o, [P, P])
    o = at("lev", o, [P, 6, P])
    o = at("small", o, [P, P])
    o = at("cols", o, [P, P])
    o = at("ones", o, [P, P])
    o = at("before", o, [P, P])
    o = at("zero", o, [P, P])
    o = at("state", o, [HD, GW])
    o = at("kc", o, [P, 32])
    o = at("vc", o, [P, HD])
    o = at("wr", o, [P, KT, 20])
    o = at("wrA", o, [P, KT, 20])
    o = at("rb", o, [P, 20])
    o = at("jm", o, [P, 4])
    o = at("e128", o, [P, E])
    o = at("jm_i", o, [P, 4], I32)
    o = at("e128_i", o, [P, E], I32)
    o = at("cnt_i", o, [P, 16], I32)
    o = at("tok", o, [P, ST])
    o = at("tok_i", o, [P, ST], I32)
    o = at("row_n", o, [P, P])
    o = at("row_i", o, [P, P], I32)
    o = at("tile_n", o, [P, E + EXTRA])
    o = at("tile_i", o, [P, E + EXTRA], I32)
    at("acc1", o, [P, 512])
    o = at("u", o, [P, GW])
    o = at("vnew", o, [P, GW])
    o = at("wpool", o, [P, 2, HD])
    o = at("st", o, [P, 768])
    assert o <= 229368 - base, o
    return tensors


def build(nc, A, out):
    ctx = ExitStack()
    T = sbuf_map(nc)

    n_st = [0]

    def stat(name, *shape, parts=P):
        w = 1
        for x in shape:
            w *= x
        v = T["st"][0:parts, n_st[0]:n_st[0] + w]
        n_st[0] += w
        assert n_st[0] <= 768, name
        if len(shape) == 2:
            v = v.rearrange("p (a b) -> p a b", a=shape[0])
        if len(shape) == 3:
            v = v.rearrange("p (a b c) -> p a b c", a=shape[0], b=shape[1])
        return v

    cT, csil = stat("cT", KT), stat("csil", KT)
    mod = stat("mod", 48)
    A1, A2 = stat("A1", KT), stat("A2", KT)
    ss, rstd = stat("ss", ST), stat("rstd", ST)
    ss2, rstd2 = stat("ss2", ST), stat("rstd2", ST)
    sinkb, alogb, dtb = stat("sinkb", H), stat("alogb", H), stat("dtb", H)
    nsink = stat("nsink", H)
    beta, sp1, sp2, ga = (stat(n, ST, H) for n in ("beta", "sp1", "sp2", "ga"))
    negA = stat("negA", H)
    sqk, rqk = stat("sqk", ST, 8), stat("rqk", ST, 8)
    egc, kdec, rqe, rkbe, rkd = (stat(n, ST, H) for n in ("egc", "kdec", "rqe", "rkbe", "rkd"))
    cdec = stat("cdec", NCH, H)
    gate = stat("gate", ST, 12)
    sso, rso = stat("sso", ST, H), stat("rso", ST, H)
    poolrec = stat("poolrec", 16)
    nm = stat("nm", 2)
    den = stat("den", 2)
    rden = stat("rden", 2)
    esk = stat("esk", 2)
    one = stat("one", 1)

    PS = [ctx.enter_context(nc.psum_tensor(f"ps{i}", [P, 512], F32)) for i in range(8)]
    sems = {}
    dve_link, pool_link = [None], [None]

    def sem(name):
        if name not in sems:
            sems[name] = ctx.enter_context(nc.semaphore(name))
        return sems[name]

    W = T["win"]
    CC = (T["cc"], T["cc1"])
    idf, idb, cols = T["idf"], T["idb"], T["cols"]

    def in_cols(name, a=0, n=P):
        return lambda k: W[:, k, OFF[name] + a:OFF[name] + a + n]

    MOVED = {"aq": ((0, 0), (2, 1), (1, 2), (3, 3)), "ckv": ((2, 2), (4, 3), (3, 4), (5, 5))}

    block = ctx.enter_context(nc.Block())

    items = []
    for c in range(6):
        items.append(("cin", c, "act"))
    for i in range(ST):
        items.append(("zba", i, "dve" if i % 2 else "act"))
    for n, (name, j) in enumerate([("kcvT", 0), ("ksw", 0), ("cqT", 0), ("cqT", 1), ("plT", 0), ("plT", 1),
                                   ("aqT", 0), ("aqT", 1), ("akT", 0)]):
        items.append((name, j, "dve" if n % 2 else "act"))
    for i in range(ST):
        items.append(("v", i, "dve" if i % 2 else "act"))
    NI = len(items)
    PB = 6
    out_count = []
    seen = {"act": 0, "dve": 0}
    for it in items:
        seen[it[2]] += 1
        out_count.append((it[2], seen[it[2]]))
    ZBA_OUT = 6 + ST - 1
    GSUM = PS[6][:, 64:128]

    def bank_empty(eng, n):
        who, k = out_count[n]
        eng.wait_ge(sem("proj_out_" + who), k)

    def all_out(eng, n):
        for who in ("act", "dve"):
            k = max([c for w, c in out_count[:n + 1] if w == who])
            eng.wait_ge(sem("proj_out_" + who), k)

    def empty_item(eng, scalar, n):
        name, j, _ = items[n]
        bank = PS[n % PB]
        signal = sem("proj_out_act" if scalar else "proj_out_dve")
        scale = 0.125 if name in ("cqT", "aqT") else 1.0
        src = bank[:, :]
        if name == "cin":
            if j >= 2:
                eng.wait_ge(sem("conv_done"), j - 1)
            dst = T["cin"][:, j % 2, CONV:CONV + S]
        elif name == "zba":
            dst, src = T["zba"][:, j, :], bank[:, 0:ZBA]
        elif name == "v":
            parts = [(T["va"][:, j, :], bank[:, 0:P]), (T["vsw"][:, j, :], bank[:, P:2 * P]),
                     (T["cg"][:, j, :], bank[:, 2 * P:2 * P + 12])]
        elif name != "ksw":
            dst = T[name][:, j, :]
        if name == "ksw":
            lo, hi = slice(0, HD), slice(HD, P)
            parts = [(T["kselT"][lo, 0, :], bank[lo, :]), (T["kselT"][hi, 0, :], bank[lo, :]),
                     (T["kwinT"][lo, 0, :], bank[hi, :]), (T["kwinT"][hi, 0, :], bank[hi, :])]
        elif name != "v":
            parts = [(dst, src)]
        for n_part, (d, s) in enumerate(parts):
            if scalar:
                ins = nc.scalar.activation(d, s, ACT.Copy, scale=scale)
            elif scale != 1.0:
                ins = nc.vector.tensor_scalar(d, s, scale, None, ALU.mult)
            else:
                ins = nc.vector.tensor_copy(d, s)
        ins.then_inc(signal, 1)

    HP_CHUNKS = 512 // P
    ada_v = A["w_ada"][0].rearrange("(p k) n -> p k n", k=KT)
    win_v = A["w_in"][0].rearrange("(k p) n -> p k n", p=P)
    WIN_GROUPS = [(OFF["dqkv"], OFF["dqkv"] + 2 * P), (OFF["dqkv"] + 2 * P, OFF["dz"]), (OFF["dz"], IN_W),
                  (OFF["ckv"], OFF["dqkv"]),
                  (OFF["cq"], OFF["ckv"]), (0, OFF["cq"])]
    GROUP_DMAS = (1, 1, 1, 6, 1, 5)
    GROUP_OF = {"cin": 1, "zba": 2, "kcvT": 3, "ksw": 3, "cqT": 4, "aqT": 5, "akT": 5, "plT": 5, "v": 5}
    HPS = 12

    def ada_slot(n):
        if n == 2:
            return T["ada2"][:], sem("ada_in2"), 16
        slot = n if n < 2 else (n + 1) % 2
        return T["ada"][:, slot], sem(f"ada_in{slot}"), 16 * max(1, (n + 1) // 2)

    groups = [("swa", h) for h in range(H)]
    for pair in range(2):
        for kind in ("cmp", "sel", "win"):
            for h in (2 * pair, 2 * pair + 1):
                groups.append((kind, h))
    units = []
    for gi, (kind, h) in enumerate(groups):
        for i in range(ST):
            j0 = max(i - 1, 0) if kind == "swa" else 0
            nk = NCMP if kind == "cmp" else (i + 1 - j0) * P
            units.append((gi, kind, h, i, j0, nk))
    NU = len(units)
    SLOTS = NU // ST
    SCORE, PROB_T, YBANK = PS[5], PS[6], PS[7]
    BANK_DONE = {1: 0, 3: 1, 9: 4, 15: 5}

    def q_of(kind, h, i):
        tok = slice(i * P, (i + 1) * P)
        if kind == "swa":
            pb = HD * (h // 2)
            return T["aqT"][pb:pb + HD, h % 2, tok], pb
        pb = HD * (h % 2)
        return T["cqT"][pb:pb + HD, h // 2, tok], pb

    def pe_compress(pe):
        t = nc.tensor
        pe.wait_ge(sem("w1_in"), 64)
        pe.wait_ge(sem("kpos"), 1)
        pe.wait_ge(sem("exp"), SLOTS)
        for l in range(CMP_LEN):
            for b in range(2):
                pb = slice(HD * b, HD * b + HD)
                ins = t.matmul(SCORE[pb, 0:NCMP], T["w1"][pb, l, :],
                               T["kpos"][pb, l // CMP_STRIDE, l:l + CMP_STRIDE * (NCMP - 1) + 1:CMP_STRIDE],
                               start=(l == 0), stop=(l == CMP_LEN - 1))
        ins.then_inc(sem("hid_mm"), 1)
        pe.wait_ge(sem("hid"), 1)
        for b in range(2):
            t.matmul(SCORE[HD * b:HD * b + HD, HD:HD + NCMP], T["w2"][0:HD], T["hid"][0:HD, 0:NCMP], start=True, stop=True)
        t.matmul(SCORE[0:NCMP, P:P + HD], T["hid"][HD:P, 0:NCMP], T["w2"][HD:P], start=True,
                 stop=True).then_inc(sem("kc_mm"), 1)
        pe.wait_ge(sem("kc_out"), 1)

    def act_compress(act):
        act.wait_ge(sem("hid_mm"), 1)
        nc.scalar.activation(T["hid"][:, 0:NCMP], SCORE[:, 0:NCMP], ACT.Silu).then_inc(sem("hid"), 1)

    def dve_compress(dve):
        v = nc.vector
        dve.wait_ge(sem("kc_mm"), 1)
        v.tensor_copy(T["kc"][:, 0:NCMP], SCORE[:, HD:HD + NCMP])
        v.tensor_copy(T["vc"][0:NCMP, :], SCORE[0:NCMP, P:P + HD]).then_inc(sem("kc_out"), 1)

    def pe_attention_step(pe, s):
        t = nc.tensor
        if s < NU:
            gi, kind, h, i, j0, nk = units[s]
            q, pb = q_of(kind, h, i)
            if kind == "cmp":
                keys = T["kc"][pb:pb + HD, 0:NCMP]
            else:
                keys = {"sel": T["kselT"], "win": T["kwinT"], "swa": T["akT"]}[kind][pb:pb + HD, 0,
                                                                                   j0 * P:j0 * P + nk]
            if s:
                pe.wait_ge(sem("exp"), s)
            t.matmul(SCORE[:, 0:nk], q, keys, start=True, stop=False)
            if kind == "cmp":
                masks = [(SCORE[:, 0:NCMP], T["negcmp"][:, i, 0, :])]
            else:
                masks = [(SCORE[:, nk - P:nk], T["negdiag"][:])]
                if kind == "swa" and i:
                    masks.append((SCORE[:, 0:P], T["negprev"][:]))
            for n, (o, m) in enumerate(masks):
                ins = t.matmul(o, idb[:], m, start=False, stop=(n == len(masks) - 1))
            ins.then_inc(sem("score_mm"), 1)
        if 2 <= s < NU + 2:
            w = s - 2
            gi, kind, h, i, j0, nk = units[w]
            pe.wait_ge(sem("prob"), w + 1)
            if w:
                pe.wait_ge(sem("pT_out"), w)
            if kind == "cmp":
                ins = t.transpose(PROB_T[0:NCMP, 0:P], T["pr"][:, w % 2, 0:NCMP], idf[:])
            else:
                for b in range(nk // P):
                    ins = t.transpose(PROB_T[:, b * P:(b + 1) * P], T["pr"][:, w % 2, b * P:(b + 1) * P], idf[:])
            ins.then_inc(sem("prob_tr"), 1)
        if 3 <= s and units[s - 3][3] == ST - 1:
            gi, kind, h = units[s - 3][:3]
            pe.wait_ge(sem("pT_out"), s - 2)
            done = [g for g in BANK_DONE if g < gi]
            if done:
                pe.wait_ge(sem("y_att"), len(done))
            y = YBANK[HD * (h % 2):HD * (h % 2) + HD]
            pT = T["pTr"][:, gi % 2]
            if kind == "cmp":
                ins = t.matmul(y[:, :], T["vc"][0:NCMP, :], pT[0:NCMP, 0, :], start=True, stop=False)
            elif kind == "swa":
                for i in range(ST):
                    js = [j for j in (i - 1, i) if j >= 0]
                    for j in js:
                        ins = t.matmul(y[:, i * P:(i + 1) * P], T["va"][:, j, HD * (h // 2):HD * (h // 2) + HD],
                                       pT[:, j, i * P:(i + 1) * P], start=(j == js[0]), stop=(j == i))
            else:
                o = 0 if kind == "sel" else HD
                for j in range(ST):
                    ins = t.matmul(y[:, j * P:S], T["vsw"][:, j, o:o + HD], pT[:, j, j * P:S], start=False,
                                   stop=(kind == "win" and j == ST - 1))
            ins.then_inc(sem("pv_mm"), 1)

    def dve_attention_start(dve):
        v = nc.vector
        v.tensor_scalar(nsink, sinkb, -1.0, None, ALU.mult).then_inc(sem("cnt"), 1)
        dve.wait_ge(sem("scalars"), 4)
        dve.wait_ge(sem("cnt"), 2)

    def dve_attention_step(dve, s):
        v = nc.vector
        link = dve_link[0]
        if s < NU:
            gi, kind, h, i, j0, nk = units[s]
            dve.wait_ge(sem("score_mm"), s + 1)
            m = nm[:, s % 2:s % 2 + 1]
            ins = v.tensor_reduce(m, SCORE[:, 0:nk], AX.X, ALU.max, negate=True)
            if kind == "swa":
                link(ins)
                ins = v.tensor_scalar(m, m, nsink[:, h:h + 1], None, ALU.min)
            if kind == "cmp":
                link(ins)
                ins = v.tensor_scalar(m, m, 1e20, None, ALU.min)
            ins.then_inc(sem("max"), 1)
        if 1 <= s < NU + 1:
            w = s - 1
            gi, kind, h, i, j0, nk = units[w]
            dve.wait_ge(sem("exp"), w + 1)
            d, r = den[:, w % 2:w % 2 + 1], rden[:, w % 2:w % 2 + 1]
            if kind == "swa":
                link(v.tensor_tensor(d, d, esk[:, w % 2:w % 2 + 1], ALU.add))
            if kind == "cmp":
                link(v.tensor_scalar(d, d, 0.5, None, ALU.max))
            link(v.reciprocal(r, d))
            p = T["pr"][:, w % 2, 0:nk]
            if kind == "swa":
                ins = v.tensor_scalar(p, p, r, None, ALU.mult)
            else:
                b = 3 * h + {"cmp": 0, "sel": 1, "win": 2}[kind]
                ins = v.tensor_scalar(p, p, r, gate[:, i, b:b + 1], ALU.mult, ALU.mult)
            ins.then_inc(sem("prob"), 1)
        if 3 <= s and units[s - 3][3] == ST - 1 and units[s - 3][0] in BANK_DONE:
            gi = units[s - 3][0]
            dve.wait_ge(sem("pv_mm"), gi + 1)
            v.tensor_copy(T["yT"][:, BANK_DONE[gi], :], YBANK[:, :]).then_inc(sem("y_att"), 1)

    def act_attention_step(act, s):
        a = nc.scalar
        if s < NU:
            gi, kind, h, i, j0, nk = units[s]
            if s == 0:
                act.wait_ge(sem("sq_sum"), 2)
                act.wait_ge(sem("ada_used"), HPS)
            act.wait_ge(sem("max"), s + 1)
            if s >= 2:
                act.wait_ge(sem("prob_tr"), s - 1)
            m = nm[:, s % 2:s % 2 + 1]
            if kind == "swa":
                a.activation(esk[:, s % 2:s % 2 + 1], sinkb[:, h:h + 1], ACT.Exp, bias=m)
            a.activation(T["pr"][:, s % 2, 0:nk], SCORE[:, 0:nk], ACT.Exp, bias=m,
                         accum_out=den[:, s % 2:s % 2 + 1]).then_inc(sem("exp"), 1)
        if 2 <= s < NU + 2:
            w = s - 2
            gi, kind, h, i, j0, nk = units[w]
            act.wait_ge(sem("prob_tr"), w + 1)
            if i == 0 and gi >= 2:
                act.wait_ge(sem("pv_mm"), gi - 1)
            tok = slice(i * P, (i + 1) * P)
            if kind == "cmp":
                ins = a.activation(T["pTr"][0:NCMP, gi % 2, 0, tok], PROB_T[0:NCMP, 0:P], ACT.Copy)
            else:
                nb = nk // P
                ins = a.activation(T["pTr"][:, gi % 2, j0:j0 + nb, tok],
                                   PROB_T[:, 0:nk].rearrange("p (j c) -> p j c", j=nb), ACT.Copy)
            ins.then_inc(sem("pT_out"), 1)

    def pe_pool_products(pe):
        t = nc.tensor
        pe.wait_ge(sem("pool_d"), 4)
        pe.wait_ge(sem("exp"), NU)
        for c in range(2):
            for b in range(2):
                pb = slice(HD * b, HD * b + HD)
                ins = t.matmul(PS[2 + 2 * c + b][pb, :], T["wpool"][pb, c, :], T["pd"][pb, c, :], start=True, stop=True)
        ins.then_inc(sem("pool_mm"), 1)

    def dve_pool_output(dve):
        v = nc.vector
        dve.wait_ge(sem("pool_mm"), 1)
        for c in range(2):
            for b in range(2):
                pb = slice(HD * b, HD * b + HD)
                v.tensor_scalar(T["yT"][pb, 2 + c, :], PS[2 + 2 * c + b][pb, :], cols[pb, 64 + c:65 + c], None,
                                ALU.mult).then_inc(sem("y_out"), 1)

    def act_dn_norm(act):
        act.wait_ge(sem("var"), 3)
        nc.scalar.activation(rso, sso, ACT.Sqrt).then_inc(sem("sd"), 1)

    def pool_compress(pool):
        g = nc.gpsimd
        all_out(pool, NI - 1)
        x = T["kcvT"][:, 0, :].rearrange("p (n l) -> p n l", l=CMP_STRIDE)
        for b in range(2):
            pos = cols[:, 91 + CMP_STRIDE * b:91 + CMP_STRIDE * (b + 1)]
            ins = g.tensor_tensor(T["kpos"][:, b, :].rearrange("p (n l) -> p n l", l=CMP_STRIDE), x,
                                  pos.unsqueeze(1).broadcast_to([P, S // CMP_STRIDE, CMP_STRIDE]), ALU.add)
        ins.then_inc(sem("kpos"), 1)

    def pool_windows(pool, n):
        g = nc.gpsimd
        link = pool_link[0]
        pool.wait_ge(sem("cc"), 5 * (n + 1))
        x, d = T["plT"], T["pd"]
        dst = T["pb"] if n % 2 else T["pa"]
        src = (T["pa"] if n % 2 else T["pb"]) if n else x
        if n == 0:
            pool.wait_ge(sem("ada_used"), HPS)
            all_out(pool, NI - 1)
        w = POOLW[n]
        s = w // 2
        for p0, p1, c in (((0, P, 0), (0, P, 1)), ((HD, P, 0), (0, P, 1)), ((0, P, 1),), ((HD, P, 1),))[n]:
            g.tensor_copy(dst[p0:p1, c, 0:s], src[p0:p1, c, 0:s])
            link(g.tensor_tensor(dst[p0:p1, c, s:S], src[p0:p1, c, s:S], src[p0:p1, c, 0:S - s], ALU.add))
        p0, p1, c = HD * (n % 2), HD * (n % 2) + HD, n // 2
        pool.wait_ge(sem("cnt"), 1)
        link(g.tensor_scalar(d[p0:p1, c, w:S], dst[p0:p1, c, w:S], 1.0 / w, 0.0, ALU.mult, ALU.add))
        link(g.tensor_tensor(d[p0:p1, c, 0:w], dst[p0:p1, c, 0:w], poolrec[p0:p1, 0:w], ALU.mult))
        g.tensor_tensor(d[p0:p1, c, :], d[p0:p1, c, :], x[p0:p1, c, :], ALU.subtract).then_inc(sem("pool_d"), 1)
        pool.wait_ge(sem("pool_d"), n + 1)
    xn2_d = nc.dram_tensor("xn2_rows", [S, D], F32).ap()
    yo_d = nc.dram_tensor("expert_rows", [ROWS, D], F32).ap()
    wg_v, wu_v = (A[n][0].rearrange("g e (k p) f -> (g e) p k f", p=P) for n in ("w_gate", "w_up"))
    wd_v = A["w_down"][0].rearrange("g e (k p) d -> (g e) p k d", p=P)
    gu, dn = (T["gu0"], T["gu1"]), (T["dn0"], T["dn1"])
    NPAIR = E // 2

    def load_gate_up(q, e, b):
        for n, v in enumerate((wg_v, wu_v)):
            q.dma_start(gu[b][:, n], v[e]).then_inc(sem(f"gu_in{b}"), 16)

    def load_down(q, e, b):
        q.dma_start(dn[b][:], wd_v[e]).then_inc(sem(f"dn_in{b}"), 16)

    def sync_moe(sp):
        sp.wait_ge(sem("scan_end"), ST)
        sp.wait_ge(sem("scan_mm"), NCH)
        sp.dma_start(T["xr"][:], A["x"][0].rearrange("(i p) d -> p i d", p=P)).then_inc(sem("xr_in"), 16)
        sp.wait_ge(sem("y_out"), 6)
        sp.wait_ge(sem("y_att"), 4)
        load_gate_up(sp, 0, 0)
        load_down(sp, 0, 0)
        for i in range(ST):
            if i == 3:
                sp.wait_ge(sem("oproj_mm"), ST)
                load_gate_up(sp, 1, 1)
            sp.wait_ge(sem("xn2"), i + 1)
            sp.dma_start(xn2_d[i * P:(i + 1) * P, :], T["xn2"][:, i % 2, :]).then_inc(sem(f"xn2_st{i % 2}"), 16)
        sp.dma_start(T["fnb"][:], A["final_norm"].partition_broadcast(P)).then_inc(sem("fn_in"), 16)
        with sp.Fori(0, NPAIR - 1) as j:
            for b in range(2):
                sp.wait_ge(sem("gu_mm"), j * 2 + (b + 1))
                load_gate_up(sp, j * 2 + (b + 2), b)
        sp.wait_ge(sem("route_i"), 1)
        n_extra = sp.value_load(T["route_i"][0:1, 0:1], min_val=0, max_val=EXTRA)
        for x in range(EXTRA):
            with sp.If(n_extra > x):
                e = sp.value_load(T["route_i"][0:1, 1 + x:2 + x], min_val=0, max_val=E - 1)
                sp.wait_ge(sem("dn_mm"), E + x)
                load_gate_up(sp, e, 0)
                load_down(sp, e, 0)
        for i in range(ST):
            sp.wait_ge(sem("final"), i + 1)
            sp.dma_start(out[0, i * P:(i + 1) * P, :], T["x2"][:, i, :]).then_inc(sem("out_st"), 16)
        sp.wait_ge(sem("out_st"), 16 * ST)

    def pe_rows(pe, n, b, came):
        pe.wait_ge(sem(f"xg_in{b}"), came)
        pe.wait_ge(sem("xgT_a"), n)
        pe.wait_ge(sem("xgT_d"), n)
        for k in range(KT):
            ins = nc.tensor.transpose(PS[6 + k // 4][:, (k % 4) * P:(k % 4 + 1) * P],
                                      T["xg"][:, b, k * P:(k + 1) * P], idf[:])
        ins.then_inc(sem("xg_tr"), 1)

    def pe_gate_up(pe, n, b, came):
        pe.wait_ge(sem(f"gu_in{b}"), came)
        pe.wait_ge(sem("xgT_a"), n + 1)
        pe.wait_ge(sem("xgT_d"), n + 1)
        for k in range(KT):
            for w in range(2):
                ins = nc.tensor.matmul(PS[2 * b + w][:, :], T["xgT"][:, k, :], gu[b][:, w, k, :], start=(k == 0),
                                       stop=(k == KT - 1))
        ins.then_inc(sem("gu_mm"), 1)

    def pe_hidden(pe, n, b):
        pe.wait_ge(sem("hidm"), n + 1)
        for f in range(FT):
            ins = nc.tensor.transpose(PS[2 * b][:, f * P:(f + 1) * P], T["hidm"][:, f * P:(f + 1) * P], idf[:])
        ins.then_inc(sem("hid_tr"), 1)

    def pe_down(pe, n, b, came):
        pe.wait_ge(sem("hidT"), n + 1)
        pe.wait_ge(sem(f"dn_in{b}"), came)
        pe.wait_ge(sem("yo_d"), n + 1)
        for f in range(FT):
            for w in range(2):
                ins = nc.tensor.matmul(PS[4 + w][:, :], T["hidT"][:, f, :], dn[b][:, f, w * 512:(w + 1) * 512],
                                       start=(f == 0), stop=(f == FT - 1))
        ins.then_inc(sem("dn_mm"), 1)

    def act_rows(act, n):
        act.wait_ge(sem("xg_tr"), n + 1)
        for k in range(4):
            ins = nc.scalar.activation(T["xgT"][:, k, :], PS[6][:, k * P:(k + 1) * P], ACT.Identity,
                                       scale=A2[:, k:k + 1], bias=mod[:, 24 + k:25 + k])
        ins.then_inc(sem("xgT_a"), 1)

    def act_silu(act, n, b):
        act.wait_ge(sem("gu_mm"), n + 1)
        nc.scalar.activation(T["sg"][:], PS[2 * b][:, :], ACT.Silu).then_inc(sem("sg"), 1)

    def act_hidden(act, n, b):
        act.wait_ge(sem("hid_tr"), n + 1)
        nc.scalar.activation(T["hidT"][:].rearrange("p a b -> p (a b)"), PS[2 * b][:, :],
                             ACT.Copy).then_inc(sem("hidT"), 1)

    def act_output(act, n):
        act.wait_ge(sem("yo_d"), n + 2)
        act.dma_start(yo_d.rearrange("(t p) d -> t p d", p=P)[n], T["yo"][:]).then_inc(sem("yo_st"), 16)

    def dve_rows(dve, n):
        dve.wait_ge(sem("xg_tr"), n + 1)
        for k in range(4, KT):
            ins = nc.vector.tensor_scalar(T["xgT"][:, k, :], PS[7][:, (k - 4) * P:(k - 3) * P], A2[:, k:k + 1],
                                          mod[:, 24 + k:25 + k], ALU.mult, ALU.add)
        ins.then_inc(sem("xgT_d"), 1)

    def dve_product(dve, n, b):
        dve.wait_ge(sem("sg"), n + 1)
        nc.vector.tensor_tensor(T["hidm"][:], T["sg"][:], PS[2 * b + 1][:, :], ALU.mult).then_inc(sem("hidm"), 1)

    def dve_output(dve, n):
        dve.wait_ge(sem("dn_mm"), n + 1)
        dve.wait_ge(sem("yo_st"), n * 16 + 16)
        for w in range(2):
            c = slice(w * 512, (w + 1) * 512)
            ins = nc.vector.tensor_tensor(T["yo"][:, c], PS[4 + w][:, :], T["g2b"][:, c], ALU.mult)
        ins.then_inc(sem("yo_d"), 1)

    def extras(eng, body):
        eng.wait_ge(sem("route_i"), 1)
        n_extra = eng.value_load(T["route_i"][0:1, 0:1], min_val=0, max_val=EXTRA)
        for x in range(EXTRA):
            with eng.If(n_extra > x):
                body(x, E + x)

    Y_ORDER = (0, 1, 4, 5, 2, 3, 6, 7)

    def output_products(i, ks):
        for k in ks:
            for n in range(2):
                ins = nc.tensor.matmul(PS[2 * (i % 2) + n][:, :], T["yT"][:, k, i * P:(i + 1) * P],
                                       T["wout"][:, k, n * 512:(n + 1) * 512], start=(k == Y_ORDER[0]),
                                       stop=(k == Y_ORDER[-1]))
        return ins

    def pe_output_start(pe):
        pe.wait_ge(sem("wout_in"), 16)
        pe.wait_ge(sem("wT_out"), ST)
        pe.wait_ge(sem("o_out"), ST)
        pe.wait_ge(sem("y_att"), 4)
        output_products(0, Y_ORDER[:4])
        pe.wait_ge(sem("y_out"), 4)
        output_products(0, Y_ORDER[4:KT - 2])

    def pe_moe(pe):
        t = nc.tensor
        pe.wait_ge(sem("wr_in"), 64)
        pe.wait_ge(sem("y_out"), 6)
        pe.wait_ge(sem("y_att"), 4)
        for k in range(KT):
            t.matmul(PS[7][:, 80:100], mod[:, 24 + k:25 + k].broadcast_to([P, P]), T["wr"][:, k, :], start=(k == 0),
                     stop=(k == KT - 1))
        for i in range(ST + 1):
            if i < ST:
                if i >= 2:
                    pe.wait_ge(sem("x2"), i - 1)
                output_products(i, Y_ORDER if i else Y_ORDER[KT - 2:]).then_inc(sem("oproj_mm"), 1)
            if i >= 1:
                w = i - 1
                pe.wait_ge(sem("x2"), w + 1)
                if w:
                    pe.wait_ge(sem("x2T"), 2 * w)
                for k in range(KT):
                    ins = t.transpose(PS[4 + k // 4][:, (k % 4) * P:(k % 4 + 1) * P],
                                      T["x2"][:, w, k * P:(k + 1) * P], idf[:])
                ins.then_inc(sem("x2_tr"), 1)
                pe.wait_ge(sem("x2T"), 2 * w + 2)
                pe.wait_ge(sem("wrA"), 1)
                lg = PS[7][:, w * 20:w * 20 + 20]
                for k in range(KT):
                    ins = t.matmul(lg, T["x2T"][:, k, :], T["wrA"][:, k, :], start=(k == 0), stop=(k == KT - 1))
                ins.then_inc(sem("logit_mm"), 1)
        pe.wait_ge(sem("chosen"), 1)
        ch = T["chosen"]
        rank = PS[6][:, 0:(ST + 1) * E]
        t.matmul(rank, T["before"][:], ch[:].rearrange("p i e -> p (i e)"), start=True, stop=False)
        for i in range(1, ST + 1):
            n = ST + 1 - i
            ins = t.matmul(PS[6][:, i * E:(ST + 1) * E], T["ones"][:], ch[:, 0:n, :].rearrange("p i e -> p (i e)"),
                           start=False, stop=(i == ST))
        ins.then_inc(sem("rank_mm"), 1)
        pe.wait_ge(sem("places"), 1)
        for n in range(2):
            for i in range(ST):
                ins = t.matmul(PS[6][:, P:P + E + EXTRA], T["in_row"][:, n, i, :], T["in_tile"][:, n, i, :],
                               start=(n + i == 0), stop=(n == 1 and i == ST - 1))
        ins.then_inc(sem("list_mm"), 1)
        pe.wait_ge(sem("list"), 1)
        pe_rows_first(pe)
        pe_gate_up(pe, 0, 0, 32)
        pe_rows(pe, 1, 1, 16)
        with pe.Fori(0, NPAIR - 1) as j:
            for n, b in ((j * 2 + 1, 1), (j * 2 + 2, 0)):
                pe_hidden(pe, n - 1, 1 - b)
                pe_gate_up(pe, n, b, j * 32 + (32 if b else 64))
                pe_rows(pe, n + 1, 1 - b, j * 16 + 32)
                pe_down(pe, n - 1, 1 - b, j * 16 + 16)
        pe_hidden(pe, E - 2, 0)
        pe_gate_up(pe, E - 1, 1, 32 * NPAIR)
        pe_down(pe, E - 2, 0, 16 * NPAIR)
        pe_hidden(pe, E - 1, 1)
        pe_down(pe, E - 1, 1, 16 * NPAIR)

        def extra(x, n):
            pe_rows(pe, n, 0, 16 * (NPAIR + x + 1))
            pe_gate_up(pe, n, 0, 32 * (NPAIR + x + 1))
            pe_hidden(pe, n, 0)
            pe_down(pe, n, 0, 16 * (NPAIR + x + 1))

        extras(pe, extra)

    def pe_rows_first(pe):
        pe.wait_ge(sem("xg_in0"), 16)
        for k in range(KT):
            ins = nc.tensor.transpose(PS[6 + k // 4][:, (k % 4) * P:(k % 4 + 1) * P], T["xg"][:, 0, k * P:(k + 1) * P],
                                      idf[:])
        ins.then_inc(sem("xg_tr"), 1)

    def act_moe(act):
        a = nc.scalar
        for i in range(ST):
            act.wait_ge(sem("x2"), i + 1)
            if i:
                act.wait_ge(sem("ss"), ST + i)
            a.activation(T["sqs"][:], T["x2"][:, i, :], ACT.Square, accum_out=ss2[:, i:i + 1]).then_inc(sem("ss"), 1)
            act.wait_ge(sem("var"), 3 + i + 1)
            a.activation(rstd2[:, i:i + 1], ss2[:, i:i + 1], ACT.Sqrt).then_inc(sem("sd"), 1)
            act.wait_ge(sem("x2_tr"), i + 1)
            if i:
                act.wait_ge(sem("logit_mm"), i)
            for n in range(2):
                a.activation(T["x2T"][:, 4 * n:4 * n + 4, :].rearrange("p a b -> p (a b)"), PS[4 + n][:, :],
                             ACT.Copy).then_inc(sem("x2T"), 1)
        act.wait_ge(sem("exp_in"), 1)
        a.activation(T["eg"][:], T["eg"][:], ACT.Exp).then_inc(sem("exp_out"), 1)
        act.wait_ge(sem("exp_in"), 2)
        a.activation(T["ed"][:], T["ed"][:], ACT.Exp).then_inc(sem("exp_out"), 1)
        load_down(act, 1, 1)
        act_rows(act, 0)
        act_silu(act, 0, 0)
        act_rows(act, 1)
        with act.Fori(0, NPAIR - 1) as j:
            for n, b in ((j * 2 + 1, 1), (j * 2 + 2, 0)):
                act_hidden(act, n - 1, 1 - b)
                act_silu(act, n, b)
                act_rows(act, n + 1)
                act_output(act, n - 1)
                load_down(act, n + 1, 1 - b)
        act_hidden(act, E - 2, 0)
        act_silu(act, E - 1, 1)
        act_output(act, E - 2)
        act_hidden(act, E - 1, 1)
        act_output(act, E - 1)

        act.wait_ge(sem("yo_zero"), 16 * EXTRA)

        def extra(x, n):
            act_rows(act, n)
            act_silu(act, n, 0)
            act_hidden(act, n, 0)
            act_output(act, n)

        extras(act, extra)
        for i in range(ST):
            act.wait_ge(sem("x3"), i + 1)
            if i:
                act.wait_ge(sem("ss"), 2 * ST + i)
            a.activation(T["sqs"][:], T["x2"][:, i, :], ACT.Square, accum_out=ss[:, i:i + 1]).then_inc(sem("ss"), 1)
            act.wait_ge(sem("var"), 3 + ST + i + 1)
            a.activation(rstd[:, i:i + 1], ss[:, i:i + 1], ACT.Sqrt).then_inc(sem("sd"), 1)

    def dve_moe(dve):
        v = nc.vector
        link = dve_link[0]
        dve.wait_ge(sem("wr_in"), 64)
        v.tensor_tensor(T["wrA"][:], T["wr"][:], A2.unsqueeze(2).broadcast_to([P, KT, 20]),
                        ALU.mult).then_inc(sem("wrA"), 1)
        dve.wait_ge(sem("gb"), 4)
        for i in range(ST):
            dve.wait_ge(sem("oproj_mm"), i + 1)
            dve.wait_ge(sem("xr_in"), 16)
            for n in range(2):
                link(v.tensor_tensor(T["x2"][:, i, n * 512:(n + 1) * 512], PS[2 * (i % 2) + n][:, :],
                                     T["g1b"][:, n * 512:(n + 1) * 512], ALU.mult))
            v.tensor_tensor(T["x2"][:, i, :], T["x2"][:, i, :], T["xr"][:, i], ALU.add).then_inc(sem("x2"), 1)
            c = slice(i, i + 1)
            dve.wait_ge(sem("ss"), ST + i + 1)
            v.tensor_scalar(ss2[:, c], ss2[:, c], 1.0 / D, EPS, ALU.mult, ALU.add).then_inc(sem("var"), 1)
            dve.wait_ge(sem("sd"), 3 + i + 1)
            link(v.reciprocal(rstd2[:, c], rstd2[:, c]))
            if i >= 2:
                dve.wait_ge(sem(f"xn2_st{i % 2}"), 16)
            v.tensor_scalar(T["xn2"][:, i % 2, :], T["x2"][:, i, :], rstd2[:, c], None, ALU.mult).then_inc(sem("xn2"), 1)
        dve.wait_ge(sem("logit_mm"), ST)
        lg = T["lg"]
        link(v.memset(T["chosen"][:, ST, :], 0.0))
        link(v.tensor_tensor(T["rb"][:], T["rb"][:], PS[7][:, 80:100], ALU.add))
        for i in range(ST):
            ins = v.scalar_tensor_tensor(lg[:, i, :], PS[7][:, i * 20:(i + 1) * 20], rstd2[:, i:i + 1], T["rb"][:],
                                         ALU.mult, ALU.add)
        link(ins)
        rg, mx, t4, mn, jm = lg[:, :, 0:G], T["mx"][:], T["t4"][:], T["mn"][:], T["jm"][:]

        def wide(x, n=4):
            return x.unsqueeze(2).broadcast_to([P, ST, n])

        def top(src, first):
            link(v.tensor_reduce(mx, src, AX.X, ALU.max))
            link(v.tensor_tensor(t4, src, wide(mx), ALU.is_equal))
            link(v.tensor_tensor(t4, t4, jm.unsqueeze(1).broadcast_to([P, ST, 4]), ALU.mult))
            link(v.tensor_reduce(mn, t4, AX.X, ALU.min))
            link(v.tensor_tensor(first, jm.unsqueeze(1).broadcast_to([P, ST, 4]), wide(mn), ALU.is_equal))

        ohg, oh1, oh2, le, m1 = (T[n][:] for n in ("ohg", "oh1", "oh2", "le", "m1"))
        top(rg, ohg)
        v.tensor_tensor(T["eg"][:], rg, wide(mx), ALU.subtract).then_inc(sem("exp_in"), 1)
        e16 = T["e16"]
        e4 = e16[:].rearrange("p i (g e) -> p i g e", g=G)
        link(v.tensor_tensor(e4, lg[:, :, G:20].rearrange("p i (g e) -> p i g e", g=G),
                             ohg.unsqueeze(3).broadcast_to([P, ST, G, EG]), ALU.mult))
        link(v.tensor_reduce(le, e16[:].rearrange("p i (g e) -> p i e g", g=G), AX.X, ALU.add))
        top(le, oh1)
        link(v.tensor_copy(m1, mx))
        link(v.scalar_tensor_tensor(le, oh1, NEG, le, ALU.mult, ALU.add))
        top(le, oh2)
        v.tensor_tensor(T["ed"][:], mx, m1, ALU.subtract).then_inc(sem("exp_in"), 1)
        for n, (o, oh) in enumerate((("M1", oh1), ("M2", oh2))):
            link(v.tensor_tensor(T[o][:].rearrange("p i (g e) -> p i g e", g=G),
                                 ohg.unsqueeze(3).broadcast_to([P, ST, G, EG]),
                                 oh.unsqueeze(2).broadcast_to([P, ST, G, EG]), ALU.mult))
        v.tensor_tensor(T["chosen"][:, 0:ST], T["M1"][:], T["M2"][:], ALU.add).then_inc(sem("chosen"), 1)
        dve.wait_ge(sem("rank_mm"), 1)
        rank, cnt, xe, t16, incl, bb = (T[n][:] for n in ("rank", "count", "xe", "t16", "incl", "bb"))
        link(v.tensor_copy(rank, PS[6][:, 0:ST * E].rearrange("p (i e) -> p i e", i=ST)))
        link(v.tensor_copy(cnt, PS[6][:, ST * E:(ST + 1) * E]))
        link(v.tensor_scalar(xe, cnt, float(P), None, ALU.is_gt))
        for m in (2, 3):
            link(v.tensor_scalar(t16, cnt, float(m * P), None, ALU.is_gt))
            link(v.tensor_tensor(xe, xe, t16, ALU.add))
        link(v.memset(t16, 0.0))
        link(v.tensor_tensor_scan(incl, xe, t16, 0.0, ALU.add, ALU.add))
        link(v.tensor_tensor(bb, incl, xe, ALU.subtract))
        link(v.tensor_scalar(bb, bb, float(E - 1), float(P), ALU.add, ALU.mult))
        e128 = T["e128"][:]
        link(v.tensor_tensor(bb, bb, e128, ALU.subtract))
        r16 = T["r16"][:]
        link(v.tensor_scalar(e16[:], rank, float(P), None, ALU.is_ge))
        link(v.scalar_tensor_tensor(r16, e16[:], -float(P), rank, ALU.mult, ALU.add))
        for m in (2, 3):
            link(v.tensor_scalar(T["s16"][:], rank, float(m * P), None, ALU.is_ge))
            link(v.scalar_tensor_tensor(r16, T["s16"][:], -float(P), r16, ALU.mult, ALU.add))
        link(v.tensor_tensor(e16[:], e16[:], bb.unsqueeze(1).broadcast_to([P, ST, E]), ALU.mult))
        link(v.tensor_tensor(e16[:], e16[:], rank, ALU.add))
        link(v.tensor_tensor(e16[:], e16[:], e128.unsqueeze(1).broadcast_to([P, ST, E]), ALU.add))
        for n, m in enumerate(("M1", "M2")):
            link(v.tensor_tensor(T["s16"][:], e16[:], T[m][:], ALU.mult))
            link(v.tensor_reduce(T["slotf"][:, n, :], T["s16"][:], AX.X, ALU.add))
            link(v.tensor_tensor(T["s16"][:], r16, T[m][:], ALU.mult))
            link(v.tensor_reduce(T["place"][:, n, :], T["s16"][:], AX.X, ALU.add))
        link(v.tensor_tensor(T["first"][:], T["slotf"][:], T["place"][:], ALU.subtract))
        for n in range(2):
            for i in range(ST):
                v.tensor_scalar(T["in_row"][:, n, i, :], T["row_n"][:], T["place"][:, n, i:i + 1], None, ALU.is_equal)
                ins = v.tensor_scalar(T["in_tile"][:, n, i, :], T["tile_n"][:], T["first"][:, n, i:i + 1],
                                      T["tok"][:, i:i + 1], ALU.is_equal, ALU.mult)
        ins.then_inc(sem("places"), 1)
        v.tensor_copy(T["slot"][:], T["slotf"][:]).then_inc(sem("slots"), 1)
        dve.wait_ge(sem("list_mm"), 1)
        v.tensor_copy(T["list"][:], PS[6][:, P:P + E + EXTRA]).then_inc(sem("list"), 1)
        w1, w2, ed = T["w1t"][:], T["w2t"][:], T["ed"][:]
        dve.wait_ge(sem("exp_out"), 1)
        link(v.tensor_reduce(w1, T["eg"][:], AX.X, ALU.add))
        dve.wait_ge(sem("exp_out"), 2)
        link(v.scalar_tensor_tensor(w1, ed, 1.0, w1, ALU.add, ALU.mult))
        link(v.reciprocal(w1, w1))
        v.tensor_tensor(w2, w1, ed, ALU.mult).then_inc(sem("w12"), 1)
        link(v.tensor_copy(T["rf"][:, 0:1], incl[:, E - 1:E]))
        for x in range(EXTRA):
            link(v.tensor_scalar(t16, incl, float(x), None, ALU.is_le))
            link(v.tensor_reduce(T["rf"][:, 1 + x:2 + x], t16, AX.X, ALU.add))
        link(v.tensor_scalar(T["rf"][:, 1:8], T["rf"][:, 1:8], float(E - 1), None, ALU.min))
        v.tensor_copy(T["route_i"][:], T["rf"][:]).then_inc(sem("route_i"), 1)
        v.memset(T["yo"][:, 0:1], 0.0).then_inc(sem("yo_d"), 1)
        v.memset(T["yo"][:, 1:2], 0.0).then_inc(sem("yo_st"), 16)
        dve_rows(dve, 0)
        dve_product(dve, 0, 0)
        dve_rows(dve, 1)
        with dve.Fori(0, NPAIR - 1) as j:
            for n, b in ((j * 2 + 1, 1), (j * 2 + 2, 0)):
                dve_product(dve, n, b)
                dve_rows(dve, n + 1)
                dve_output(dve, n - 1)
        dve_product(dve, E - 1, 1)
        dve_output(dve, E - 2)
        dve_output(dve, E - 1)

        def extra(x, n):
            dve_rows(dve, n)
            dve_product(dve, n, 0)
            dve_output(dve, n)

        extras(dve, extra)
        dve.wait_ge(sem("fn_in"), 16)
        dve.wait_ge(sem("w12"), 1)
        for i in range(ST + 1):
            c = slice(i, i + 1)
            if i < ST:
                y, x = T["y1"][:, i, :], T["x2"][:, i, :]
                dve.wait_ge(sem(f"y_in{i}"), 32)
                link(v.scalar_tensor_tensor(x, y, w1[:, c], x, ALU.mult, ALU.add))
                v.scalar_tensor_tensor(x, T["y2"][:, i, :], w2[:, c], x, ALU.mult, ALU.add).then_inc(sem("x3"), 1)
            if not i:
                continue
            i -= 1
            c, x = slice(i, i + 1), T["x2"][:, i, :]
            dve.wait_ge(sem("ss"), 2 * ST + i + 1)
            v.tensor_scalar(ss[:, c], ss[:, c], 1.0 / D, EPS, ALU.mult, ALU.add).then_inc(sem("var"), 1)
            dve.wait_ge(sem("sd"), 3 + ST + i + 1)
            link(v.reciprocal(rstd[:, c], rstd[:, c]))
            v.scalar_tensor_tensor(x, x, rstd[:, c], T["fnb"][:], ALU.mult, ALU.mult).then_inc(sem("final"), 1)

    def pool_moe(pool):
        g = nc.gpsimd
        at = bass.IndirectOffsetOnAxis
        pool.wait_ge(sem("list"), 1)
        for b in range(2):
            pool.wait_ge(sem(f"xn2_st{b}"), 32)

        def gather(n):
            g.indirect_dma_start(T["xg"][:, n % 2 if n < E else 0, :], None, xn2_d,
                                 at(ap=T["list"][:, n:n + 1], axis=0)).then_inc(
                sem(f"xg_in{n % 2 if n < E else 0}"), 16)

        for n in range(E):
            if n >= 2:
                pool.wait_ge(sem("xg_tr"), n - 1)
            gather(n)

        def extra(x, n):
            pool.wait_ge(sem("xg_tr"), n)
            gather(n)
            pool.wait_ge(sem("yo_st"), 16 * (n + 2))

        pool.wait_ge(sem("yo_st"), 16 * (E + 1))
        pool.wait_ge(sem("slots"), 1)
        extras(pool, extra)
        for i in range(ST):
            for n, y in enumerate(("y1", "y2")):
                g.indirect_dma_start(T[y][:, i, :], None, yo_d,
                                     at(ap=T["slot"][:, n, i:i + 1], axis=0)).then_inc(sem(f"y_in{i}"), 16)

    @block.sync
    def _(sp):
        def load_ada(n):
            if n >= 3:
                sp.wait_ge(sem("ada_used"), {3: 1, 4: 2}.get(n, n - 1))
            to, signal, _ = ada_slot(n)
            sp.dma_start(to, ada_v[:, :, n * 512:(n + 1) * 512]).then_inc(signal, 16)

        sp.dma_start(cT, A["c"][0].rearrange("(p k) -> p k", k=KT)).then_inc(sem("c_in"), 16)
        for n in range(2):
            sp.dma_start(T["x"][:, 2 * n:2 * n + 2], A["x"][0].rearrange("(i p) d -> p i d", p=P)[:, 2 * n:2 * n + 2]
                         ).then_inc(sem(f"x_in{n}"), 16)
        for n in range(4):
            load_ada(n)
        for g, (a, b) in enumerate(WIN_GROUPS):
            moved = {0: "aq", OFF["ckv"]: "ckv"}.get(a)
            if moved:
                for f, to in MOVED[moved]:
                    f, to = a + HD * f, a + HD * to
                    sp.dma_start(W[:, :, to:to + HD], win_v[:, :, f:f + HD]).then_inc(sem(f"win_in{g}"), 16)
                if moved == "ckv":
                    sp.dma_start(W[:, :, a:a + P], win_v[:, :, a:a + P]).then_inc(sem(f"win_in{g}"), 16)
                a += IN_SIZES[moved]
            sp.dma_start(W[:, :, a:b], win_v[:, :, a:b]).then_inc(sem(f"win_in{g}"), 16)
        sp.wait_ge(sem("xT"), KT)
        for name, o in (("g1b", 2 * D), ("g2b", 5 * D)):
            sp.dma_start(T[name][:], A["b_ada"][0, o:o + D].partition_broadcast(P)).then_inc(sem("gb_in"), 16)
        for n in range(4, HPS):
            load_ada(n)
        sp.wait_ge(sem("proj_mm"), NI)
        w1v = A["cmp_w1"][0].rearrange("b (l d) e -> b d l e", d=HD)
        sp.dma_start(T["w1"][0:HD], w1v[0]).then_inc(sem("w1_in"), 16)
        sp.dma_start(T["w1"][HD:P], w1v[1]).then_inc(sem("w1_in"), 16)
        sp.dma_start(T["w2"][0:HD], A["cmp_w2"][0, 0]).then_inc(sem("w1_in"), 16)
        sp.dma_start(T["w2"][HD:P], A["cmp_w2"][0, 1]).then_inc(sem("w1_in"), 16)
        sp.wait_ge(sem("kc_out"), 1)
        sp.dma_start(T["wout"][:], A["w_out"][0].rearrange("(k p) n -> p k n", p=P)).then_inc(sem("wout_in"), 16)
        sync_moe(sp)

    @block.gpsimd
    def _(pool):
        link = pool_link[0] = Link(pool, sem("pool_step"))
        g = nc.gpsimd

        def select(t, pattern, base, cm, fill, op=ALU.is_ge):
            link(g.affine_select(out=t, in_=t, pattern=pattern, compare_op=op, fill=fill, base=base,
                                 channel_multiplier=cm))

        for t in (idf[:], idb[:]):
            link(g.memset(t, 0.0))
            select(t, [[-1, P]], 0, 1, 1.0, ALU.not_equal)
        link(g.memset(T["ones"][:], 1.0))
        g.memset(one, 1.0).then_inc(sem("ident"), 1)
        for t, v in ((T["negdiag"], 0.0), (T["negprev"], 0.0), (T["negcmp"], 0.0), (T["negdec"], 0.0),
                     (T["tri"], 1.0), (T["sl"], 1.0), (T["lev"], 1.0)):
            link(g.memset(t[:], v))
        select(T["negdiag"][:], [[-1, P]], 0, 1, NEG)
        select(T["negprev"][:], [[1, P]], -1, -1, NEG)
        for i in range(ST):
            select(T["negcmp"][:, i], [[0, 2], [-CMP_STRIDE, NCMP]], P * i - CMP_LEN + 1, 1, NEG)
        select(T["negdec"][:], [[0, H], [-1, P]], 0, 1, NEG)
        v = T["negdec"][:].rearrange("p h (b r) -> p h b r", b=2)
        select(v, [[0, H], [CH, 2], [0, CH]], CH - 1, -1, NEG)
        select(T["tri"][:], [[1, P]], 0, -1, 0.0)
        select(T["tri"][:].rearrange("p (b r) -> p b r", b=2), [[-CH, 2], [0, CH]], 0, 1, 0.0)
        select(T["sl"][:], [[-1, P]], -1, 1, 0.0)
        select(T["sl"][:].rearrange("p (b r) -> p b r", b=2), [[CH, 2], [0, CH]], CH - 1, -1, 0.0)
        for lv in range(6):
            s = 1 << lv
            nb = P // (2 * s)
            v = T["lev"][:, lv, :].rearrange("p (b h r) -> p b h r", h=2, r=s)
            select(v, [[-2 * s, nb], [0, 2], [0, s]], -s, 1, 0.0)
            select(v, [[2 * s, nb], [0, 2], [0, s]], 2 * s - 1, -1, 0.0)
            select(v, [[0, nb], [-1, 2], [0, s]], 0, 0, 0.0)
        link(g.memset(T["before"][:], 1.0))
        select(T["before"][:], [[1, P]], -1, -1, 0.0)
        link(g.iota(T["cnt_i"][:], pattern=[[1, 16]], base=1, channel_multiplier=0))
        link(g.iota(T["jm_i"][:], pattern=[[1, 4]], base=-16, channel_multiplier=0))
        link(g.iota(T["e128_i"][:], pattern=[[P, E]], base=0, channel_multiplier=0))
        link(g.iota(T["tok_i"][:], pattern=[[P, ST]], base=0, channel_multiplier=1))
        link(g.iota(T["row_i"][:], pattern=[[1, P]], base=0, channel_multiplier=0))
        g.iota(T["tile_i"][:], pattern=[[P, E + EXTRA]], base=0, channel_multiplier=0).then_inc(sem("masks"), 1)
        link(g.tensor_copy(poolrec, T["cnt_i"][:]))
        link(g.tensor_copy(T["jm"][:], T["jm_i"][:]))
        link(g.tensor_copy(T["e128"][:], T["e128_i"][:]))
        pool.wait_ge(sem("masks"), 1)
        for n in ("tok", "row", "tile"):
            link(g.tensor_copy(T[n if n == "tok" else n + "_n"][:], T[n + "_i"][:]))
        g.memset(T["state"][:], 0.0).then_inc(sem("masks"), 1)

        pool.wait_ge(sem("A1"), 1)
        for k in range(1, KT, 2):
            pool.wait_ge(sem("xT_out"), k + 1)
            g.tensor_scalar(T["hT"][:, k, :], T["hT"][:, k, :], A1[:, k:k + 1], mod[:, k:k + 1],
                            ALU.mult, ALU.add).then_inc(sem("hT_pool"), 1)

        link(g.memset(T["zero"][:], 0.0))
        for x in range(EXTRA):
            r = (E + x) * P
            g.dma_start(yo_d[r:r + P, :].rearrange("p (a b) -> p a b", b=P),
                        T["zero"][:].unsqueeze(1).broadcast_to([P, D // P, P])).then_inc(sem("yo_zero"), 16)
        pool.wait_ge(sem("dtok_out"), 6)
        for n in range(2):
            x = T["dtok"][:, :, n * GW:(n + 1) * GW]
            g.tensor_tensor(T["sq"][:, n], x, x, ALU.mult).then_inc(sem("qk_sq"), 1)
        pool.wait_ge(sem("proj_mm"), NI)
        pool.wait_ge(sem("d_scales"), 1)

        def sl_decays(i):
            if i >= 1:
                pool.wait_ge(sem("dec_mm"), i)
            g.tensor_tensor(T["asl"][:], T["sl"][:].unsqueeze(1).broadcast_to([P, H, P]),
                            ga[:, i, :].unsqueeze(2).broadcast_to([P, H, P]), ALU.mult).then_inc(sem("asl"), 1)

        for i in range(ST):
            def scaled(dst, src, col):
                o = T[dst][:, i, :].rearrange("p (h d) -> p h d", h=H)
                x = T["dtok"][:, i, src * GW:(src + 1) * GW].rearrange("p (h d) -> p h d", h=H)
                return g.tensor_tensor(o, x, col.unsqueeze(2).broadcast_to([P, H, HD]), ALU.mult)
            if i == 0:
                sl_decays(0)
            scaled("kbe", 1, rkbe[:, i, :])
            scaled("kd", 1, rkd[:, i, :])
            scaled("vb", 2, beta[:, i, :]).then_inc(sem("d_tok_pool"), 1)
            if i == 0:
                pool_compress(pool)
            if i:
                sl_decays(i)
            for lv in range(1, 6):
                pool.wait_ge(sem("low"), i + 1)
                if lv >= 3:
                    pool.wait_ge(sem("y_mm"), 5 * i + lv - 2)
                elif i >= 1:
                    pool.wait_ge(sem("y_mm"), 5 * i)
                g.tensor_tensor(CC[lv % 2][:], T["low"][:], T["lev"][:, lv].unsqueeze(1).broadcast_to([P, H, P]),
                                ALU.mult).then_inc(sem("cc"), 1)
            pool_windows(pool, i)
        pool_moe(pool)

    @block.scalar
    def _(act):
        link = Link(act, sem("act_step"))
        a = nc.scalar
        act.wait_ge(sem("c_in"), 16)
        a.activation(csil, cT, ACT.Silu).then_inc(sem("csil"), 1)
        q = sem("small_in")
        act.dma_start(T["small"][0:48, :], A["b_ada"][0].rearrange("(r c) -> r c", c=P)).then_inc(q, 16)
        act.dma_start(T["small"][48:56, :], A["norm_mix"][0].rearrange("(r c) -> r c", c=P)).then_inc(q, 16)
        act.dma_start(T["small"][56:64, :], A["norm_ffn"][0].rearrange("(r c) -> r c", c=P)).then_inc(q, 16)
        act.dma_start(T["small"][64:66, :], A["pool_scale"][0].rearrange("(r c) -> r c", c=P)).then_inc(q, 16)
        act.dma_start(T["small"][66:90, :], A["conv_w"][0].rearrange("j (r c) -> (j r) c", c=P)).then_inc(q, 16)
        for b in range(2):
            act.dma_start(T["small"][90:91, HD * b:HD * b + HD], A["dn_norm"]).then_inc(q, 16)
            act.dma_start(T["small"][91:123, HD * b:HD * b + HD], A["cmp_pos"][0, b]).then_inc(q, 16)
        for i in range(ST):
            act.wait_ge(sem(f"x_in{i // 2}"), 16)
            if i:
                act.wait_ge(sem("ss"), i)
            a.activation(T["hT"][:, 0:2, :].rearrange("p a b -> p (a b)"), T["x"][:, i, :], ACT.Square,
                         accum_out=ss[:, i:i + 1]).then_inc(sem("ss"), 1)
        act.wait_ge(sem("var"), 1)
        a.activation(rstd, ss, ACT.Sqrt).then_inc(sem("sd"), 1)
        for k in range(KT):
            act.wait_ge(sem("xT"), k + 1)
            a.activation(T["hT"][:, k, :], PS[k % 4][:, :], ACT.Copy).then_inc(sem("xT_out"), 1)
        for n, (t, name) in enumerate(((sinkb, "attn_sink"), (alogb, "a_log"), (dtb, "dt_bias"))):
            act.dma_start(t, A[name][0].partition_broadcast(P)).then_inc(sem("bc_in"), 16)
        for b in range(2):
            act.dma_start(T["wpool"][HD * b:HD * b + HD],
                          A["w_pool"][0].rearrange("(c b) i o -> b i c o", b=2)[b]).then_inc(sem("bc_in"), 16)
        for c, name in ((slice(0, G), "w_route_group"), (slice(G, G + E), "w_route_expert")):
            act.dma_start(T["wr"][:, :, c], A[name][0].rearrange("(k p) e -> p k e", p=P)).then_inc(sem("wr_in"), 16)
        act.dma_start(T["rb"][:, 0:G], A["b_route_group"][0].partition_broadcast(P)).then_inc(sem("wr_in"), 16)
        act.dma_start(T["rb"][:, G:20], A["b_route_expert"][0].partition_broadcast(P)).then_inc(sem("wr_in"), 16)
        def silu_conv(c):
            act.wait_ge(sem("conv_done"), c + 1)
            a.activation(T["cout"][:, c % 2, :], T["cout"][:, c % 2, :], ACT.Silu).then_inc(sem("conv_silu"), 1)

        for n in range(NI):
            if items[n][2] == "act":
                act.wait_ge(sem("proj_mm"), n + 1)
                empty_item(act, True, n)
            if 2 <= n < 8:
                silu_conv(n - 2)
            if n == ZBA_OUT:
                all_out(act, ZBA_OUT)
                act.wait_ge(sem("bc_in"), 80)
                zb = T["zba"]
                a.activation(beta, zb[:, :, GW:GW + H], ACT.Sigmoid).then_inc(sem("scalars"), 1)
                a.activation(zb[:, :, 0:GW], zb[:, :, 0:GW], ACT.Silu).then_inc(sem("scalars"), 1)
                a.activation(negA, alogb, ACT.Exp).then_inc(sem("scalars"), 1)
            if n == ZBA_OUT + 1:
                act.wait_ge(sem("sp_abs"), 1)
                link(a.activation(sp2, sp2, ACT.Exp))
                act.wait_ge(sem("ident"), 1)
                a.activation(sp2, sp2, ACT.Ln, bias=one).then_inc(sem("sp_ln"), 1)
            if n == ZBA_OUT + 4:
                act.wait_ge(sem("sq_sum"), 2)
                act.wait_ge(sem("var"), 2)
                a.activation(rqk, sqk, ACT.Sqrt).then_inc(sem("sd"), 1)
                act.wait_ge(sem("g_mm"), 1)
                a.activation(egc.rearrange("p a b -> p (a b)"), GSUM[:, 0:16], ACT.Exp)
                a.activation(kdec.rearrange("p a b -> p (a b)"), GSUM[:, 16:32], ACT.Exp)
                cv = cdec.rearrange("p (i f) h -> p f i h", f=2)
                for hf in range(2):
                    ins = a.activation(cv[0:HD, hf],
                                       GSUM[0:HD, 32 + 16 * hf:48 + 16 * hf].rearrange("p (i h) -> p i h", i=ST), ACT.Exp)
                ins.then_inc(sem("g_exp"), 1)
        all_out(act, NI - 1)
        a.activation(gate, T["cg"][:], ACT.Sigmoid).then_inc(sem("scalars"), 1)
        for i in range(ST):
            act.wait_ge(sem("qk_tr"), i + 1)
            if i:
                act.wait_ge(sem("scan_mm"), NCH // ST * i)
            a.activation(T["qT"][:].rearrange("p a b -> p (a b)"), PS[3][0:HD, :], ACT.Copy)
            a.activation(T["qdT"][:].rearrange("p a b -> p (a b)"), PS[0][0:HD, :], ACT.Copy).then_inc(sem("qT_out"), 1)
            act_attention_step(act, SLOTS * i)
            act.wait_ge(sem("dec_mm"), i + 1)
            a.activation(T["dec"][:].rearrange("p a b -> p (a b)"), PS[2][:, :], ACT.Exp).then_inc(sem("dec"), 1)
            act_attention_step(act, SLOTS * i + 1)
            act_attention_step(act, SLOTS * i + 2)
            act.wait_ge(sem("uu_tr"), i + 1)
            a.activation(T["uu"][:].rearrange("p a b -> p (a b)"), PS[4][:, :], ACT.Copy).then_inc(sem("uu0"), 1)
            act.wait_ge(sem("inT_tr"), i + 1)
            a.activation(T["inT"][:].rearrange("p a b -> p (a b)"), PS[0][:, :], ACT.Copy).then_inc(sem("inT_out"), 1)
            for lv in range(1, 6):
                act.wait_ge(sem("y_mm"), 5 * i + lv)
                a.activation(T["yy"][:].rearrange("p a b -> p (a b)"), PS[1][:, :], ACT.Copy).then_inc(sem("yy"), 1)
                for n in (1, 2):
                    act_attention_step(act, SLOTS * i + 2 * lv + n)
            act.wait_ge(sem("w_mm"), i + 1)
            a.activation(T["wT"][:].rearrange("p a b -> p (a b)"), PS[0][0:HD, :], ACT.Copy).then_inc(sem("wT_out"), 1)
            for n in range(13, SLOTS):
                act_attention_step(act, SLOTS * i + n)
            act.wait_ge(sem("scan_end"), i + 1)
            a.activation(T["osb"][:, i, :], PS[1][:, 0:GW], ACT.Copy).then_inc(sem("o_out"), 1)
            if i == 0:
                act_compress(act)
        for s in range(NU, NU + 3):
            act_attention_step(act, s)
        act_dn_norm(act)
        act_moe(act)

    GB = {4: ("g1b", 0), 5: ("g1b", 1), 10: ("g2b", 0), 11: ("g2b", 1)}

    @block.vector
    def _(dve):
        v = nc.vector
        link = dve_link[0] = Link(dve, sem("dve_step"))
        def ada_sum(n):
            o = T[f"acc{n % 2}"][:]
            piece, signal, came = ada_slot(n)
            dve.wait_ge(signal, came)
            if n >= 2:
                dve.wait_ge(sem("ada_mm"), n - 1)
            link(v.tensor_scalar(o, piece[:, 0, :], csil[:, 0:1], None, ALU.mult))
            for k in range(1, KT):
                ins = v.scalar_tensor_tensor(o, piece[:, k, :], csil[:, k:k + 1], o, ALU.mult, ALU.add)
                if k < KT - 1:
                    link(ins)
            ins.then_inc(sem("ada_used"), 1)

        dve.wait_ge(sem("ss"), ST)
        v.tensor_scalar(ss, ss, 1.0 / D, EPS, ALU.mult, ALU.add).then_inc(sem("var"), 1)
        dve.wait_ge(sem("sd"), 1)
        link(v.reciprocal(rstd, rstd))
        for i in range(ST):
            v.tensor_scalar(T["xn"][:, i, :], T["x"][:, i, :], rstd[:, i:i + 1], None, ALU.mult).then_inc(sem("xn"), 1)
        dve.wait_ge(sem("csil"), 1)
        for n in range(4):
            if n == 2:
                dve.wait_ge(sem("small_tr"), 1)
                v.tensor_copy(cols[:, 0:123], PS[7][:, 0:123]).then_inc(sem("cols"), 1)
            ada_sum(n)
        dve.wait_ge(sem("ada_mm"), 4)
        dve.wait_ge(sem("cols"), 1)
        link(v.tensor_tensor(mod[:, 0:16], PS[6][:, 0:16], cols[:, 0:16], ALU.add))
        v.scalar_tensor_tensor(A1, mod[:, 8:16], 1.0, cols[:, 48:56], ALU.add, ALU.mult).then_inc(sem("A1"), 1)
        dve.wait_ge(sem("A1"), 1)
        dve.wait_ge(sem("xT_out"), KT)
        for k in range(0, KT, 2):
            v.tensor_scalar(T["hT"][:, k, :], T["hT"][:, k, :], A1[:, k:k + 1], mod[:, k:k + 1],
                            ALU.mult, ALU.add).then_inc(sem("hT_dve"), 1)
        for b in range(2):
            dve.wait_ge(sem("xT"), KT)
            v.memset(T["cin"][:, b, 0:CONV], 0.0).then_inc(sem("cin_pad"), 1)
        dve.wait_ge(sem("masks"), 2)
        v.reciprocal(poolrec, poolrec).then_inc(sem("cnt"), 1)

        def conv(c):
            dve.wait_ge(sem("proj_out_act"), c + 1)
            dve.wait_ge(sem("cin_pad"), 2)
            if c >= 2:
                dve.wait_ge(sem("conv_tr"), c - 1)
            x, y = T["cin"], T["cout"][:, c % 2, :]
            w = [cols[:, 66 + 6 * j + c:67 + 6 * j + c] for j in range(CONV)]
            link(v.tensor_scalar(y, x[:, c % 2, CONV:CONV + S], w[3], None, ALU.mult))
            for j in range(CONV - 1):
                ins = v.scalar_tensor_tensor(y, x[:, c % 2, 1 + j:1 + j + S], w[j], y, ALU.mult, ALU.add)
                if j < CONV - 2:
                    link(ins)
            ins.then_inc(sem("conv_done"), 1)

        def log_decays_in():
            all_out(dve, ZBA_OUT)
            dve.wait_ge(sem("bc_in"), 80)
            za = T["zba"][:, :, GW + H:GW + 2 * H]
            link(v.tensor_tensor(sp1, za, dtb.unsqueeze(1).broadcast_to([P, ST, H]), ALU.add))
            v.scalar_tensor_tensor(sp2, sp1, -1.0, sp1, ALU.mult, ALU.min).then_inc(sem("sp_abs"), 1)

        def log_decays():
            dve.wait_ge(sem("sp_ln"), 1)
            link(v.scalar_tensor_tensor(sp1, sp1, 0.0, sp2, ALU.max, ALU.add))
            dve.wait_ge(sem("scalars"), 3)
            v.scalar_tensor_tensor(ga, sp1, -1.0, negA.unsqueeze(1).broadcast_to([P, ST, H]), ALU.mult,
                                   ALU.mult).then_inc(sem("ga"), 1)

        def square_sums():
            dve.wait_ge(sem("qk_sq"), 2)
            for n in range(2):
                v.tensor_reduce(sqk[:, :, 4 * n:4 * n + 4], T["sq"][:, n].rearrange("p i (h d) -> p i h d", h=H),
                                AX.X, ALU.add).then_inc(sem("sq_sum"), 1)
            dve.wait_ge(sem("sq_sum"), 2)
            v.tensor_scalar(sqk, sqk, 1e-6, None, ALU.add).then_inc(sem("var"), 1)

        rq, rk = rqk[:, :, 0:4], rqk[:, :, 4:8]

        def token_scales():
            dve.wait_ge(sem("sd"), 2)
            link(v.reciprocal(rqk, rqk))
            link(v.tensor_scalar(rq, rq, 0.125, None, ALU.mult))
            dve.wait_ge(sem("g_exp"), 1)
            dve.wait_ge(sem("scalars"), 1)
            link(v.tensor_tensor(rqe, rq, egc, ALU.mult))
            link(v.tensor_tensor(rkd, rk, kdec, ALU.mult))
            link(v.tensor_tensor(rkbe, rk, egc, ALU.mult))
            v.tensor_tensor(rkbe, rkbe, beta, ALU.mult).then_inc(sem("d_scales"), 1)

        for n in range(NI):
            if items[n][2] == "dve":
                dve.wait_ge(sem("proj_mm"), n + 1)
                empty_item(dve, False, n)
            if n < 6:
                conv(n)
            if 3 <= n < 9:
                c = n - 3
                dve.wait_ge(sem("conv_tr"), c + 1)
                v.tensor_copy(T["dtok"][:, :, c * P:(c + 1) * P],
                              PS[6 + c % 2][:, :].rearrange("p (i c) -> p i c", i=ST)).then_inc(sem("dtok_out"), 1)
            step = {ZBA_OUT: log_decays_in, ZBA_OUT + 2: log_decays, ZBA_OUT + 3: square_sums,
                    ZBA_OUT + 5: token_scales}.get(n)
            if step:
                step()
            if 10 <= n < 18 and n - 10 + 4 in GB:
                hp = n - 10 + 4
                name, half = GB[hp]
                dve.wait_ge(sem("ada_mm"), hp + 1)
                dve.wait_ge(sem("gb_in"), 32)
                o = T[name][:, half * 512:(half + 1) * 512]
                v.tensor_tensor(o, PS[7][:, :], o, ALU.add).then_inc(sem("gb"), 1)
            if 7 <= n < 15:
                ada_sum(n - 7 + 4)
        dve.wait_ge(sem("ada_mm"), 10)
        link(v.tensor_tensor(mod[:, 24:40], PS[6][:, 24:40], cols[:, 24:40], ALU.add))
        link(v.scalar_tensor_tensor(A2, mod[:, 32:40], 1.0, cols[:, 56:64], ALU.add, ALU.mult))
        dve.wait_ge(sem("proj_mm"), NI)
        dve.wait_ge(sem("d_scales"), 1)
        for i in range(ST):
            for n, (dst, src, col) in enumerate((("qn", 0, rq), ("qd", 0, rqe), ("kn", 1, rk))):
                o = T[dst][:, i, :].rearrange("p (h d) -> p h d", h=H)
                x = T["dtok"][:, i, src * GW:(src + 1) * GW].rearrange("p (h d) -> p h d", h=H)
                ins = v.tensor_tensor(o, x, col[:, i, :].unsqueeze(2).broadcast_to([P, H, HD]), ALU.mult)
            ins.then_inc(sem("d_tok_dve"), 1)
        dve_attention_start(dve)
        low, tt, uu, yy = (T[n] for n in ("low", "tt", "uu", "yy"))

        def flat(t):
            return t[:].rearrange("p a b -> p (a b)")

        def output_squares(i):
            dve.wait_ge(sem("o_out"), i + 1)
            o = T["osb"][:, i, :]
            link(v.tensor_tensor(T["qd"][:, i, :], o, o, ALU.mult))
            link(v.tensor_reduce(sso[:, i, :], T["qd"][:, i, :].rearrange("p (h d) -> p h d", h=H), AX.X, ALU.add))
            link(v.tensor_tensor(o, o, T["zba"][:, i, 0:GW], ALU.mult))

        for i in range(ST):
            dve.wait_ge(sem("qk_tr"), i + 1)
            if i:
                dve.wait_ge(sem("kk_mm"), 2 * i)
            v.tensor_copy(flat(T["kT"]), PS[4][0:HD, :]).then_inc(sem("kT_out"), 1)
            if i:
                output_squares(i - 1)
            for n in (0, 1):
                dve_attention_step(dve, SLOTS * i + n)
            dve.wait_ge(sem("dec"), i + 1)
            dve.wait_ge(sem("kk_mm"), 2 * i + 1)
            for h in range(H):
                ins = v.scalar_tensor_tensor(low[:, h, :], PS[1][:, h * P:(h + 1) * P], beta[:, i, h:h + 1],
                                             T["dec"][:, h, :], ALU.mult, ALU.mult)
            ins.then_inc(sem("low"), 1)
            dve.wait_ge(sem("low"), i + 1)
            link(v.scalar_tensor_tensor(tt[:], low[:], -1.0, T["lev"][:, 0].unsqueeze(1).broadcast_to([P, H, P]),
                                        ALU.mult, ALU.mult))
            v.tensor_tensor(tt[:], tt[:], idf[:].unsqueeze(1).broadcast_to([P, H, P]), ALU.add).then_inc(sem("tt"), 1)
            dve.wait_ge(sem("kk_mm"), 2 * i + 2)
            v.tensor_tensor(flat(T["dec"]), PS[3][:, :], flat(T["dec"]), ALU.mult).then_inc(sem("intra"), 1)
            dve_attention_step(dve, SLOTS * i + 2)
            for lv in range(1, 6):
                dve_attention_step(dve, SLOTS * i + 2 * lv + 1)
                dve.wait_ge(sem("du_mm"), 5 * i + lv)
                v.tensor_tensor(flat(uu), flat(uu), PS[3][:, :], ALU.subtract).then_inc(sem("uu"), 1)
                if lv < 5:
                    dve.wait_ge(sem("dt_mm"), 4 * i + lv)
                    v.tensor_tensor(flat(tt), flat(tt), PS[2][:, :], ALU.subtract).then_inc(sem("tt"), 1)
                dve_attention_step(dve, SLOTS * i + 2 * lv + 2)
            dve.wait_ge(sem("w_mm"), i + 1)
            if i:
                dve.wait_ge(sem("scan_mm"), 2 * i)
            v.tensor_copy(T["u"][:], PS[1][:, 0:GW]).then_inc(sem("u_out"), 1)
            dve.wait_ge(sem("u_out"), i + 1)
            link(v.tensor_copy(T["vnew"][:], T["u"][:]))
            dve_attention_step(dve, SLOTS * i + 13)
            for hf in range(2):
                c = 2 * i + hf
                pb = slice(CH * hf, CH * hf + CH)
                if c == 0:
                    v.tensor_copy(T["vnew"][pb], T["u"][pb]).then_inc(sem("vnew"), 1)
                else:
                    dve.wait_ge(sem("vn_mm"), c)
                    v.tensor_tensor(T["vnew"][pb], T["u"][pb], PS[1][pb, GW:2 * GW], ALU.subtract).then_inc(sem("vnew"), 1)
                if c < NCH - 1:
                    st = T["state"][:].rearrange("p (h d) -> p h d", h=H)
                    dve.wait_ge(sem("scan_mm"), c + 1)
                    link(v.tensor_tensor(st, st, cdec[0:HD, c, :].unsqueeze(2).broadcast_to([HD, H, HD]), ALU.mult))
                    v.tensor_tensor(T["state"][:], T["state"][:], PS[2][0:HD, 0:GW], ALU.add).then_inc(sem("state"), 1)
                dve_attention_step(dve, SLOTS * i + 14 + hf)
            if i == 0:
                dve_compress(dve)
        for s in range(NU, NU + 3):
            dve_attention_step(dve, s)
        output_squares(ST - 1)
        v.tensor_scalar(sso, sso, 1.0 / HD, EPS, ALU.mult, ALU.add).then_inc(sem("var"), 1)
        dve_pool_output(dve)
        dve.wait_ge(sem("sd"), 3)
        link(v.reciprocal(rso, rso))
        for i in range(ST):
            o = T["osb"][:, i, :].rearrange("p (h d) -> p h d", h=H)
            v.tensor_tensor(o, o, rso[:, i, :].unsqueeze(2).broadcast_to([P, H, HD]), ALU.mult).then_inc(sem("o_tok"), 1)
        for c in range(2):
            dve.wait_ge(sem("o_tr"), c + 1)
            v.tensor_scalar(T["yT"][:, 6 + c, :], PS[6 + c][:, :], cols[:, 90:91], None, ALU.mult).then_inc(sem("y_out"), 1)
        dve_moe(dve)

    @block.tensor
    def _(pe):
        t = nc.tensor
        pe.wait_ge(sem("ident"), 1)
        for k in range(KT):
            pe.wait_ge(sem("xn"), ST)
            if k >= 4:
                pe.wait_ge(sem("xT_out"), k - 3)
            for i in range(ST):
                ins = t.transpose(PS[k % 4][:, i * P:(i + 1) * P], T["xn"][:, i, k * P:(k + 1) * P], idf[:])
            ins.then_inc(sem("xT"), 1)
        pe.wait_ge(sem("small_in"), 16 * 9)
        t.transpose(PS[7][:, 0:123], T["small"][0:123, :], idf[0:123, 0:123]).then_inc(sem("small_tr"), 1)

        def ada(hp):
            pe.wait_ge(sem("ada_used"), hp + 1)
            acc = T[f"acc{hp % 2}"][:]
            if hp in GB:
                if hp > 4:
                    pe.wait_ge(sem("gb"), {5: 1, 10: 2, 11: 3}[hp])
                ins = t.matmul(PS[7][:, :], T["ones"][:], acc, start=True, stop=True)
            else:
                for c in range(HP_CHUNKS):
                    ins = t.matmul(PS[6][:, 4 * hp + c:4 * hp + c + 1], acc[:, c * P:(c + 1) * P],
                                   T["ones"][:, 0:1], start=True, stop=True)
            ins.then_inc(sem("ada_mm"), 1)

        for hp in range(4):
            ada(hp)
        for n, (name, j, _) in enumerate(items):
            group = GROUP_OF[name] if n >= 2 else 0
            pe.wait_ge(sem(f"win_in{group}"), 16 * GROUP_DMAS[group])
            if n == 0:
                pe.wait_ge(sem("hT_dve"), KT // 2)
                pe.wait_ge(sem("hT_pool"), KT // 2)
            if n >= PB:
                bank_empty(pe, n - PB)
            bank = PS[n % PB]
            if name in ("zba", "v"):
                tok = slice(j * P, (j + 1) * P)
                if name == "zba":
                    cuts = [(bank[:, 0:ZBA], lambda k: W[:, k, OFF["dz"]:OFF["dz"] + ZBA])]
                else:
                    cuts = [(bank[:, 0:P], in_cols("av")), (bank[:, P:2 * P + 12], in_cols("ckv", 4 * HD, P + 12))]
                for o, w in cuts:
                    for k in range(KT):
                        ins = t.matmul(o, T["hT"][:, k, tok], w(k), start=(k == 0), stop=(k == KT - 1))
            else:
                w = {"cin": in_cols("dqkv", P * j), "kcvT": in_cols("ckv"), "ksw": in_cols("ckv", 2 * HD),
                     "cqT": in_cols("cq", P * j), "aqT": in_cols("aq", P * j), "akT": in_cols("ak"),
                     "plT": in_cols("pool", P * j)}[name]
                for k in range(KT):
                    ins = t.matmul(bank[:, :], w(k), T["hT"][:, k, :], start=(k == 0), stop=(k == KT - 1))
            ins.then_inc(sem("proj_mm"), 1)
            if 3 <= n < 9:
                c = n - 3
                pe.wait_ge(sem("conv_silu"), c + 1)
                if c >= 2:
                    pe.wait_ge(sem("dtok_out"), c - 1)
                for i in range(ST):
                    ins = t.transpose(PS[6 + c % 2][:, i * P:(i + 1) * P], T["cout"][:, c % 2, i * P:(i + 1) * P], idf[:])
                ins.then_inc(sem("conv_tr"), 1)
            if 9 <= n < 17:
                if n == 9:
                    pe.wait_ge(sem("dtok_out"), 6)
                if n == ZBA_OUT + 5:
                    pe.wait_ge(sem("g_exp"), 1)
                ada(n - 9 + 4)
            if n == ZBA_OUT + 4:
                pe.wait_ge(sem("ga"), 1)
                pe.wait_ge(sem("masks"), 2)
                gf = ga.rearrange("p a b -> p (a b)")
                t.matmul(GSUM[:, 0:16], T["tri"][:], gf, start=True, stop=True)
                t.matmul(GSUM[:, 16:32], T["sl"][:], gf, start=True, stop=True)
                for hf in range(2):
                    ins = t.matmul(GSUM[0:HD, 32 + 16 * hf:48 + 16 * hf],
                                   T["tri"][:, CH * hf + CH - 1:CH * hf + CH].broadcast_to([P, HD]), gf, start=True,
                                   stop=True)
                ins.then_inc(sem("g_mm"), 1)
        tt, uu, yy = T["tt"], T["uu"], T["yy"]
        blk = [slice(h * P, (h + 1) * P) for h in range(H)]
        for i in range(ST):
            if i == 0:
                all_out(pe, NI - 1)
            pe.wait_ge(sem("d_tok_dve"), i + 1)
            if i:
                pe.wait_ge(sem("qT_out"), i)
                pe.wait_ge(sem("kT_out"), i)
                pe.wait_ge(sem("wT_out"), i)
            for n, name in ((3, "qn"), (0, "qd"), (4, "kn")):
                for h in range(H):
                    ins = t.transpose(PS[n][0:HD, blk[h]], T[name][:, i, h * HD:(h + 1) * HD], idf[:])
            ins.then_inc(sem("qk_tr"), 1)
            pe_attention_step(pe, SLOTS * i)
            pe.wait_ge(sem("asl"), i + 1)
            if i:
                pe.wait_ge(sem("state"), 2 * i)
            t.matmul(PS[2][:, :], T["tri"][:], T["asl"][:].rearrange("p a b -> p (a b)"), start=True, stop=False)
            t.matmul(PS[2][:, :], idb[:], T["negdec"][:].rearrange("p a b -> p (a b)"), start=False,
                     stop=True).then_inc(sem("dec_mm"), 1)
            pe_attention_step(pe, SLOTS * i + 1)
            pe.wait_ge(sem("qT_out"), i + 1)
            pe.wait_ge(sem("kT_out"), i + 1)
            if i:
                pe.wait_ge(sem("o_out"), i)
            for h in range(H):
                ins = t.matmul(PS[1][:, blk[h]], T["kT"][:, h, :], T["kT"][:, h, :], start=True, stop=True)
            ins.then_inc(sem("kk_mm"), 1)
            for h in range(H):
                ins = t.matmul(PS[3][:, blk[h]], T["qT"][:, h, :], T["kT"][:, h, :], start=True, stop=True)
            ins.then_inc(sem("kk_mm"), 1)
            pe_attention_step(pe, SLOTS * i + 2)
            pe.wait_ge(sem("tt"), 5 * i + 1)
            for h in range(H):
                ins = t.transpose(PS[4][:, blk[h]], tt[:, h, :], idf[:])
            ins.then_inc(sem("uu_tr"), 1)
            pe.wait_ge(sem("intra"), i + 1)
            for h in range(H):
                ins = t.transpose(PS[0][:, blk[h]], T["dec"][:, h, :], idf[:])
            ins.then_inc(sem("inT_tr"), 1)
            for lv in range(1, 6):
                pe.wait_ge(sem("cc"), 5 * i + lv)
                if lv == 1:
                    pe.wait_ge(sem("uu0"), i + 1)
                else:
                    pe.wait_ge(sem("uu"), 5 * i + lv - 1)
                for h in range(H):
                    ins = t.matmul(PS[1][:, blk[h]], CC[lv % 2][:, h, :], uu[:, h, :], start=True, stop=True)
                ins.then_inc(sem("y_mm"), 1)
                pe_attention_step(pe, SLOTS * i + 2 * lv + 1)
                pe.wait_ge(sem("yy"), 5 * i + lv)
                pe.wait_ge(sem("tt"), 5 * i + lv)
                for h in range(H):
                    ins = t.matmul(PS[3][:, blk[h]], tt[:, h, :], yy[:, h, :], start=True, stop=True)
                ins.then_inc(sem("du_mm"), 1)
                if lv < 5:
                    for h in range(H):
                        ins = t.matmul(PS[2][:, blk[h]], yy[:, h, :], tt[:, h, :], start=True, stop=True)
                    ins.then_inc(sem("dt_mm"), 1)
                pe_attention_step(pe, SLOTS * i + 2 * lv + 2)
            pe.wait_ge(sem("uu"), 5 * i + 5)
            pe.wait_ge(sem("d_tok_pool"), i + 1)
            pe.wait_ge(sem("inT_out"), i + 1)
            for h in range(H):
                t.matmul(PS[0][0:HD, blk[h]], T["kbe"][:, i, h * HD:(h + 1) * HD], uu[:, h, :], start=True, stop=True)
            for h in range(H):
                ins = t.matmul(PS[1][:, h * HD:(h + 1) * HD], uu[:, h, :], T["vb"][:, i, h * HD:(h + 1) * HD],
                               start=True, stop=True)
            ins.then_inc(sem("w_mm"), 1)
            pe_attention_step(pe, SLOTS * i + 13)
            pe.wait_ge(sem("wT_out"), i + 1)
            pe.wait_ge(sem("u_out"), i + 1)
            for hf in range(2):
                c = 2 * i + hf
                pb = slice(CH * hf, CH * hf + CH)
                hd = [slice(h * HD, (h + 1) * HD) for h in range(H)]
                if c:
                    pe.wait_ge(sem("state"), c)
                    for h in range(H):
                        ins = t.matmul(PS[1][pb, GW + h * HD:GW + (h + 1) * HD], T["wT"][:, h, pb],
                                       T["state"][:, hd[h]], start=True, stop=True)
                    ins.then_inc(sem("vn_mm"), 1)
                pe.wait_ge(sem("vnew"), c + 1)
                for h in range(H):
                    t.matmul(PS[1][pb, hd[h]], T["qdT"][:, h, pb], T["state"][:, hd[h]], start=True, stop=False)
                    ins = t.matmul(PS[1][pb, hd[h]], T["inT"][:, h, pb], T["vnew"][:, hd[h]], start=False, stop=True)
                if hf:
                    ins.then_inc(sem("scan_end"), 1)
                for h in range(H):
                    ins = t.matmul(PS[2][0:HD, hd[h]], T["kd"][pb, i, hd[h]],
                                   T["vnew"][pb, hd[h]], start=True, stop=True)
                ins.then_inc(sem("scan_mm"), 1)
                pe_attention_step(pe, SLOTS * i + 14 + hf)
            if i == 0:
                pe_compress(pe)
        for s in range(NU, NU + 3):
            pe_attention_step(pe, s)
        pe_pool_products(pe)
        pe_output_start(pe)
        for i in range(ST):
            pe.wait_ge(sem("o_tok"), i + 1)
        pe.wait_ge(sem("pT_out"), NU)
        for c in range(2):
            for i in range(ST):
                ins = t.transpose(PS[6 + c][:, i * P:(i + 1) * P], T["osb"][:, i, c * P:(c + 1) * P], idf[:])
            ins.then_inc(sem("o_tr"), 1)
        pe_moe(pe)
    ctx.close()


_NAMES = ["x", "c", "norm_mix", "norm_ffn", "final_norm", "w_ada", "b_ada", "w_in", "w_out", "attn_sink", "w_pool",
          "pool_scale", "cmp_pos", "cmp_w1", "cmp_w2", "conv_w", "a_log", "dt_bias", "dn_norm", "w_route_group",
          "b_route_group", "w_route_expert", "b_route_expert", "w_gate", "w_up", "w_down"]


def kernel(**inputs):
    import numpy as np
    import concourse.bacc as bacc
    from concourse.bass_utils import run_bass_kernel_spmd

    nc = bacc.Bacc("TRN2", target_bir_lowering=False, num_devices=1)
    arrays, views = {}, {}
    for name in _NAMES:
        a = np.ascontiguousarray(inputs[name])
        arrays["in_" + name] = a
        views[name] = nc.dram_tensor("in_" + name, a.shape, mybir.dt.from_np(a.dtype), kind="ExternalInput").ap()
    out = nc.dram_tensor("out_y", (1, S, D), F32, kind="ExternalOutput").ap()
    build(nc, views, out)
    r = run_bass_kernel_spmd(nc, [arrays], core_ids=[0])
    return r.results[0]["out_y"]
```
